# Optimizing a Trainium2 kernel written in Bass

```python
import jax, jax.numpy as jnp
from jax import lax
import numpy as np

D_MODEL = 1024
BATCH = 1
SEQ = 2048
DEPTH = 2
DEC_BATCH = 1
DEC_SEQ = 32
PAST_LEN = 1024

CHUNK = 64
N_HEADS = 16
HEAD_DIM = 64
N_KV_HEADS = 4
GQA_GROUP = N_HEADS // N_KV_HEADS
ATTN_WIDTH = N_HEADS * HEAD_DIM
KV_WIDTH = N_KV_HEADS * HEAD_DIM
WINDOW = 128
WINDOW_CHUNKS = WINDOW // CHUNK
POOL_WIDTH = D_MODEL
POOL_WINDOWS = (2, 4, 8, 16)
N_POOL_GROUPS = len(POOL_WINDOWS)
POOL_GROUP_WIDTH = POOL_WIDTH // N_POOL_GROUPS
POOL_HIST = max(POOL_WINDOWS) - 1
N_POOL_LAYERS = (DEPTH + 1) // 2
N_ATTN_LAYERS = DEPTH // 2
NORM_EPS = 1e-6
MASK_VALUE = -1e30

kernel_name = "chunk_streaming_pool_swa_hybrid_step"

def rms_norm(x, g):
    xf = x.astype(jnp.float32)
    y = xf * lax.rsqrt(jnp.mean(xf * xf, axis=-1, keepdims=True) + NORM_EPS)
    return (y * g.astype(jnp.float32)).astype(x.dtype)

def alibi_slopes():
    h = jnp.arange(1, N_HEADS + 1, dtype=jnp.float32)
    return jnp.exp2(-8.0 * h / N_HEADS)

def modulation(c, w, b):
    m = jnp.einsum('bd,de->be', jax.nn.silu(c), w) + b
    return jnp.split(m, 3, axis=-1)

def multiscale_pool(u, hist, hist_pos):
    B, T, E = u.shape
    u_ext = jnp.concatenate([hist.astype(u.dtype), u], axis=1)
    valid = jnp.concatenate([(hist_pos >= 0).astype(jnp.float32), jnp.ones((T,), jnp.float32)])
    cs = jnp.concatenate([jnp.zeros((B, 1, E), jnp.float32), jnp.cumsum(u_ext.astype(jnp.float32), axis=1)], axis=1)
    cv = jnp.concatenate([jnp.zeros((1,), jnp.float32), jnp.cumsum(valid)])
    uf = u.astype(jnp.float32)
    outs = []
    for g, w in enumerate(POOL_WINDOWS):
        sl = slice(g * POOL_GROUP_WIDTH, (g + 1) * POOL_GROUP_WIDTH)
        lo = POOL_HIST + 1 - w
        s = cs[:, POOL_HIST + 1:, sl] - cs[:, lo:lo + T, sl]
        n = cv[POOL_HIST + 1:] - cv[lo:lo + T]
        outs.append(s / n[None, :, None] - uf[..., sl])
    return jnp.stack(outs, axis=2), u_ext[:, -POOL_HIST:]

def pool_mixer(h, hist, hist_pos, w_in, w_grp, scale, w_out):
    B, T, _ = h.shape
    u, gate = jnp.split(h @ w_in, 2, axis=-1)
    pooled, new_hist = multiscale_pool(u, hist, hist_pos)
    z = jnp.einsum('btgc,gcd->btgd', pooled, w_grp.astype(jnp.float32)).reshape(B, T, POOL_WIDTH)
    z = z * scale.astype(jnp.float32)
    y = (z.astype(h.dtype) * jax.nn.silu(gate)) @ w_out
    return y, new_hist

def qkv_gate(h, w_in):
    B, T, _ = h.shape
    p = h @ w_in
    q, k, v, gate = jnp.split(p, [ATTN_WIDTH, ATTN_WIDTH + KV_WIDTH, ATTN_WIDTH + 2 * KV_WIDTH], axis=-1)
    return (q.reshape(B, T, N_KV_HEADS, GQA_GROUP, HEAD_DIM),
            k.reshape(B, T, N_KV_HEADS, HEAD_DIM),
            v.reshape(B, T, N_KV_HEADS, HEAD_DIM), gate)

def band_attend(q, k, v, qpos, kpos, sinks):
    s = jnp.einsum('bnqkgd,bnskd->bnkgqs', q.astype(jnp.float32), k.astype(jnp.float32)) * (HEAD_DIM ** -0.5)
    slopes = alibi_slopes().reshape(N_KV_HEADS, GQA_GROUP)
    dist = jnp.abs(qpos[:, :, None] - kpos[:, None, :]).astype(jnp.float32)
    qc = qpos[:, :, None] // CHUNK
    kc = kpos[:, None, :] // CHUNK
    allowed = (kpos[:, None, :] >= 0) & (kc <= qc) & (kc >= qc - WINDOW_CHUNKS)
    s = s - slopes[None, None, :, :, None, None] * dist[None, :, None, None]
    s = jnp.where(allowed[None, :, None, None], s, MASK_VALUE)
    sink = sinks.astype(jnp.float32).reshape(N_KV_HEADS, GQA_GROUP)[None, None, :, :, None]
    m = jnp.maximum(jnp.max(s, axis=-1), sink)
    p = jnp.exp(s - m[..., None])
    denom = jnp.sum(p, axis=-1) + jnp.exp(sink - m)
    return jnp.einsum('bnkgqs,bnskd->bnqkgd', p / denom[..., None], v.astype(jnp.float32))

def attn_prompt(h, w_in, sinks, w_out):
    B, T, _ = h.shape
    NC = T // CHUNK
    q, k, v, gate = qkv_gate(h, w_in)
    pad = WINDOW_CHUNKS * CHUNK

    def band(a):
        ap = jnp.pad(a, ((0, 0), (pad, 0), (0, 0), (0, 0))).reshape(B, NC + WINDOW_CHUNKS, CHUNK, N_KV_HEADS, HEAD_DIM)
        return jnp.concatenate([ap[:, j:j + NC] for j in range(WINDOW_CHUNKS + 1)], axis=2)

    qb = q.reshape(B, NC, CHUNK, N_KV_HEADS, GQA_GROUP, HEAD_DIM)
    qpos = jnp.arange(T, dtype=jnp.int32).reshape(NC, CHUNK)
    kpos = jnp.concatenate([qpos + (j - WINDOW_CHUNKS) * CHUNK for j in range(WINDOW_CHUNKS + 1)], axis=1)
    o = band_attend(qb, band(k), band(v), qpos, kpos, sinks).reshape(B, T, ATTN_WIDTH)
    y = (o.astype(h.dtype) * jax.nn.silu(gate)) @ w_out
    return y, k[:, -WINDOW:], v[:, -WINDOW:]

def attn_sample(h, k_cache, v_cache, w_in, sinks, w_out):
    B, T, _ = h.shape
    L = k_cache.shape[1]
    q, k, v, gate = qkv_gate(h, w_in)
    k_all = jnp.concatenate([k_cache.astype(k.dtype), k], axis=1)
    v_all = jnp.concatenate([v_cache.astype(v.dtype), v], axis=1)
    qpos = PAST_LEN + jnp.arange(T, dtype=jnp.int32)
    kpos = jnp.concatenate([PAST_LEN - L + jnp.arange(L, dtype=jnp.int32), qpos])
    o = band_attend(q[:, None], k_all[:, None], v_all[:, None], qpos[None], kpos[None], sinks)
    o = o[:, 0].reshape(B, T, ATTN_WIDTH)
    y = (o.astype(h.dtype) * jax.nn.silu(gate)) @ w_out
    return y, k_all[:, -L:], v_all[:, -L:]

def setup_inputs(seed: int = 0) -> dict:
    key = jax.random.key(seed)
    ks = jax.random.split(key, 18)
    nrm = jax.random.normal
    f32 = jnp.float32
    return {
        "x_prompt": nrm(ks[0], (BATCH, SEQ, D_MODEL), f32),
        "x_sample": nrm(ks[1], (DEC_BATCH, DEC_SEQ, D_MODEL), f32),
        "c_prompt": nrm(ks[2], (BATCH, D_MODEL), f32),
        "c_sample": nrm(ks[3], (DEC_BATCH, D_MODEL), f32),
        "cache_pool": nrm(ks[4], (N_POOL_LAYERS, DEC_BATCH, POOL_HIST, POOL_WIDTH), f32),
        "cache_k": nrm(ks[5], (N_ATTN_LAYERS, DEC_BATCH, min(WINDOW, PAST_LEN), N_KV_HEADS, HEAD_DIM), f32),
        "cache_v": nrm(ks[6], (N_ATTN_LAYERS, DEC_BATCH, min(WINDOW, PAST_LEN), N_KV_HEADS, HEAD_DIM), f32),
        "norm_g": 1.0 + 0.1 * nrm(ks[7], (DEPTH, D_MODEL), f32),
        "ada_w": 0.5 * D_MODEL ** -0.5 * nrm(ks[8], (DEPTH, D_MODEL, 3 * D_MODEL), f32),
        "ada_b": 0.02 * nrm(ks[9], (DEPTH, 3 * D_MODEL), f32),
        "pool_w_in": D_MODEL ** -0.5 * nrm(ks[10], (N_POOL_LAYERS, D_MODEL, 2 * POOL_WIDTH), f32),
        "pool_w_grp": POOL_GROUP_WIDTH ** -0.5 * nrm(ks[11], (N_POOL_LAYERS, N_POOL_GROUPS, POOL_GROUP_WIDTH, POOL_GROUP_WIDTH), f32),
        "pool_scale": 1.0 + 0.1 * nrm(ks[12], (N_POOL_LAYERS, POOL_WIDTH), f32),
        "pool_w_out": POOL_WIDTH ** -0.5 * nrm(ks[13], (N_POOL_LAYERS, POOL_WIDTH, D_MODEL), f32),
        "attn_w_in": D_MODEL ** -0.5 * nrm(ks[14], (N_ATTN_LAYERS, D_MODEL, 2 * ATTN_WIDTH + 2 * KV_WIDTH), f32),
        "attn_sinks": nrm(ks[15], (N_ATTN_LAYERS, N_HEADS), f32),
        "attn_w_out": ATTN_WIDTH ** -0.5 * nrm(ks[16], (N_ATTN_LAYERS, ATTN_WIDTH, D_MODEL), f32),
        "final_g": 1.0 + 0.1 * nrm(ks[17], (D_MODEL,), f32),
    }

def reference(x_prompt, x_sample, c_prompt, c_sample, cache_pool, cache_k, cache_v,
              norm_g, ada_w, ada_b, pool_w_in, pool_w_grp, pool_scale, pool_w_out,
              attn_w_in, attn_sinks, attn_w_out, final_g):

    def trunk(x, c, sample):
        B = x.shape[0]
        pool_states, k_states, v_states = [], [], []
        for i in range(DEPTH):
            j = i // 2
            shift, scale, gate = modulation(c, ada_w[i], ada_b[i])
            h = rms_norm(x, norm_g[i]) * (1 + scale[:, None]) + shift[:, None]
            if i % 2 == 0:
                if sample:
                    hist = cache_pool[j]
                    hist_pos = PAST_LEN - POOL_HIST + jnp.arange(POOL_HIST, dtype=jnp.int32)
                else:
                    hist = jnp.zeros((B, POOL_HIST, POOL_WIDTH), h.dtype)
                    hist_pos = jnp.arange(POOL_HIST, dtype=jnp.int32) - POOL_HIST
                y, st = pool_mixer(h, hist, hist_pos, pool_w_in[j], pool_w_grp[j], pool_scale[j], pool_w_out[j])
                pool_states.append(st)
            else:
                if sample:
                    y, kw, vw = attn_sample(h, cache_k[j], cache_v[j], attn_w_in[j], attn_sinks[j], attn_w_out[j])
                else:
                    y, kw, vw = attn_prompt(h, attn_w_in[j], attn_sinks[j], attn_w_out[j])
                k_states.append(kw)
                v_states.append(vw)
            x = x + gate[:, None] * y
        return rms_norm(x, final_g), jnp.stack(pool_states), jnp.stack(k_states), jnp.stack(v_states)

    y_prompt, pool_p, k_p, v_p = trunk(x_prompt, c_prompt, False)
    y_sample, pool_s, k_s, v_s = trunk(x_sample, c_sample, True)
    return (y_prompt, y_sample, pool_p, k_p, v_p, pool_s, k_s, v_s)


_drawn_inputs = setup_inputs


def setup_inputs(seed=0):
    import zlib

    import numpy as np

    out = dict(_drawn_inputs(seed))
    spreads = {}
    factors = {'cache_pool': 2.731, 'pool_scale': 3.215, 'attn_sinks': 8.0}
    for name, (base, spread) in spreads.items():
        noise = np.random.default_rng([zlib.crc32(name.encode()), seed]).standard_normal(out[name].shape)
        drawn = base * np.exp(spread * noise) if base else spread * noise
        out[name] = __import__('jax').numpy.asarray(drawn.astype(out[name].dtype))
    for name, factor in factors.items():
        out[name] = (out[name] * factor).astype(out[name].dtype)
    return out
```

```python
from contextlib import ExitStack

import concourse.bass as bass
from concourse import mybir

F32 = mybir.dt.float32
F32R = mybir.dt.float32r
I32 = mybir.dt.int32
ALU = mybir.AluOpType
ACT = mybir.ActivationFunctionType
AX_X = mybir.AxisListType.X

P = 128
D_MODEL = 1024
KT = D_MODEL // P
SEQ = 2048
PART = 512
PARTS = SEQ // PART
SAMPLE = 32
COLS = PART + SAMPLE
TILES = PART // P
GROUPS = 4
WINDOWS = (2, 4, 8, 16)
HIST = 16
HEADS = 16
HEAD_DIM = 64
WINDOW = 128
EPS = 1e-6
BIG = 1e33
RING = 4
AHEAD = 2
LANDING = 4
SHIFT = 2
LOWEST = -3e38

U_PROMPT = 2 * HIST
U_SAMPLE = U_PROMPT + PART + 2 * HIST
U_COLS = U_SAMPLE + SAMPLE
S_COLS = HIST + PART + HIST + SAMPLE
K_CACHE = WINDOW + PART
K_NEW = K_CACHE + WINDOW
K_COLS = K_NEW + SAMPLE
R_ADA_B, R_NORM, R_FINAL, R_POOL, R_C, R_ALL = 0, 48, 64, 72, 80, 96


def slope(h):
    return 2.0 ** (-8.0 * (h + 1) / HEADS)


def spans(c0, w):
    out = []
    if c0 < PART:
        out.append((c0, min(w, PART - c0), 0))
    if c0 + w > PART:
        s = max(c0, PART)
        out.append((s, c0 + w - s, 1))
    return out


class Schedule:

    def __init__(self):
        self.tiles, self.units, self.items, self.steps = [], [], [], []
        self.last_unit = {}
        self.mods = [(0, 1), (0, 0), (0, 2), (1, 1), (1, 0), (1, 2)]
        self.first = 2 * KT
        self.ada_next = 0
        for p in range(PARTS):
            self.part(p)
        self.steps = [s for s in self.steps if s[0] != "W" or s[1] < len(self.tiles)]
        seen = {}
        for u in self.units:
            for kind in (u["kind"], "proj" if u["kind"] in ("u", "gate", "kv", "q", "agate") else None,
                         "anygate" if u["kind"] in ("gate", "agate") else None):
                if kind:
                    u["nth_" + kind] = seen.get(kind, 0) + 1
                    seen[kind] = seen.get(kind, 0) + 1

    def unit_group(self, p, tile, kind, **more):
        s = self.steps
        j = len(self.tiles)
        self.tiles.append(tile)
        s.append(("W", j + AHEAD))
        made = []
        for b, (c0, w) in enumerate(self.blocks(p)):
            made.append(self.unit(p, j, kind, b, c0, w, **more))
        self.last_unit[j] = made[-1]
        return made

    def ada(self, p):
        i = self.ada_next
        if p or i == KT * len(self.mods):
            return
        self.ada_next += 1
        self.steps.append(("ADA", i))
        if i % KT == KT - 1:
            self.steps.append(("MR", i // KT))
        elif i % KT == 1 and i // KT - 1 in (0, 2, 3):
            self.steps.append(("MT", i // KT - 1))

    def unit(self, p, j, kind, b, c0, w, **more):
        self.units.append(dict(u=len(self.units), p=p, j=j, kind=kind, b=b, c0=c0, w=w, **more))
        return len(self.units) - 1

    def blocks(self, p):
        return [(0, COLS // 2), (COLS // 2, COLS // 2)] if p == 0 else [(0, PART)]

    def part(self, p):
        s = self.steps
        n_tok = TILES + (p == 0)
        if p == 0:
            for t in range(2):
                s.append(("XL", p, t))
            for i in range(self.first):
                self.ada(p)
                if i % 2 == 0 and i // 2 - 1 in range(n_tok):
                    t = i // 2 - 1
                    s.append(("XT", p, t))
                    if t + 2 < n_tok:
                        s.append(("XL", p, t + 2))
                if i >= self.first - 4:
                    for k in range(2):
                        s.append(("HS", p, 2 * (i - self.first + 4) + k))
            for j in range(AHEAD):
                s.append(("W", j))
            s.append(("MT", 1))
            s.append(("SH", 0))
        else:
            for t in range(n_tok):
                s.append(("XT", p, t))
                if t + 2 < n_tok:
                    s.append(("XL", p, t + 2))
            for k in range(KT):
                s.append(("HS", p, k))
        norm = [0]

        def emit(us, kind_evacs):
            for u in us:
                s.append(("U", u))
                norm[0] += 1
                if norm[0] <= 2:
                    s.append(("NA" if norm[0] == 1 else "NB", p, layer))
                    if norm[0] == 2:
                        for x in pending:
                            s.append(x)
                        pending.clear()
                e = [(k, u) for k in kind_evacs]
                if norm[0] < 2:
                    pending.extend(e)
                else:
                    s.extend(e)

        pending = []
        layer = 0
        if 0 < p < PARTS - 1:
            for t in range(2):
                s.append(("XL", p + 1, t))
        for g in range(GROUPS):
            for i in range(2):
                emit(self.unit_group(p, ("pin", 2 * g + i), "u", n=2 * g + i, g=g, i=i), ["E1"])
                if g or i:
                    self.ada(p)
                if i == 1:
                    s.append(("PL", p, g, 0))
            late = []
            for i in range(2):
                us = self.unit_group(p, ("pin", KT + 2 * g + i), "gate", n=KT + 2 * g + i, g=g, i=i)
                for u in us:
                    s.append(("U", u))
                    if i == 0:
                        if u == us[0]:
                            s.append(("PL", p, g, 1))
                    s.extend(late)
                    late = [("E2", u)]
                    s.append(("E1", u))
                self.ada(p)
            if g:
                self.ada(p)
            j = len(self.tiles)
            self.tiles.append(("grp", g))
            s.append(("W", j + AHEAD))
            for m in range(2):
                for b, (c0, w) in enumerate(self.blocks(p)):
                    u = self.unit(p, j, "z", b, c0, w, n=2 * g + m, g=g, m=m)
                    s.append(("U", u))
                    s.extend(late)
                    late = [("E1", u)]
                    self.last_unit[j] = u
            s.extend(late)
        if p in (0, PARTS - 1):
            s.append(("PS", p))
        late = []
        if p == 0:
            while self.ada_next < 5 * KT:
                self.ada(p)
            s.append(("MT", 4))
            s.append(("SH", 1))
        for n in range(KT):
            for u in self.unit_group(p, ("pout", n), "out", n=n, layer=0):
                s.append(("U", u))
                s.append(("E1", u))
                s.extend(late)
                late = [("E2", u)]
            self.ada(p)
        s.extend(late)
        if p == 0:
            s.append(("MT", 5))
            for t in range(2):
                s.append(("XL", p + 1, t))
        norm[0], layer = 0, 1
        kinds = [(0, 1), (2, 3)] + ([(4,)] if p == 0 else [])
        queue = []

        def item(g, hp, tiles):
            a = len(self.items)
            self.items.append(dict(a=a, p=p, g=g, hp=hp, tiles=tiles, sample=tiles == (4,)))
            return a

        def tick(a):
            if a is not None:
                if self.items[a]["tiles"][0] in (0,):
                    s.append(("BI", p, self.items[a]["g"], self.items[a]["hp"]))
                s.append(("S", a))
                s.append(("SM", a))
            queue.append(a)
            if len(queue) >= 2 and queue[-2] is not None:
                s.append(("TR", queue[-2]))
                s.append(("SPL", queue[-2]))
            if len(queue) >= 3 and queue[-3] is not None:
                s.append(("PV", queue[-3]))
                s.append(("OG", queue[-3]))

        waiting = []
        for g in range(GROUPS):
            emit(self.unit_group(p, ("kv", g), "kv", n=2 * KT + 5 * g, g=g), ["E1"])
            if waiting:
                for a in waiting[:len(kinds) - 1]:
                    tick(a)
            late_kv = [("KS", p, g)]
            us = self.unit_group(p, ("ain", 256 * g), "q", n=2 * KT + 5 * g + 1, g=g, i=0)
            emit(us, ["E1", "E2"])
            s.extend(late_kv)
            s.append(("VT", p, g))
            if waiting:
                for a in waiting[len(kinds) - 1:]:
                    tick(a)
            us = self.unit_group(p, ("ain", 256 * g + P), "q", n=2 * KT + 5 * g + 2, g=g, i=1)
            emit(us, ["E1", "E2"])
            first = [item(g, 0, t) for t in kinds]
            for a in first[:len(kinds) - 1]:
                tick(a)
            for i in range(2):
                us = self.unit_group(p, ("ain", 1536 + 256 * g + P * i), "agate",
                                     n=2 * KT + 5 * g + 3 + i, g=g, i=i)
                emit(us, ["E1", "E2"])
                if i == 0:
                    for a in first[len(kinds) - 1:]:
                        tick(a)
            waiting = [item(g, 1, t) for t in kinds]
        for a in waiting:
            tick(a)
        tick(None)
        tick(None)
        late = []
        for n in range(KT):
            for u in self.unit_group(p, ("aout", n), "out", n=n, layer=1):
                s.append(("U", u))
                s.append(("E1", u))
        s.append(("NA", p, 2))
        for t in range(n_tok):
            s.append(("FT", p, t))


def trunk_kernel(nc, I, O):
    sched = Schedule()
    tiles, units, items, steps = sched.tiles, sched.units, sched.items, sched.steps

    with ExitStack() as ctx:
        def sb(name, shape, dt=F32):
            return ctx.enter_context(nc.sbuf_tensor(name, shape, dt))

        def ps(name, shape):
            return ctx.enter_context(nc.psum_tensor(name, shape, F32))

        def sem(name):
            return ctx.enter_context(nc.semaphore(name))

        x_res = sb("x_res", [P, KT, COLS])
        h_all_hi = sb("h_all_hi", [P, KT, SHIFT + COLS], F32R)
        h_all_lo = sb("h_all_lo", [P, KT, SHIFT + COLS], F32R)
        y_hi, y_lo = sb("y_hi", [P, KT, COLS], F32R), sb("y_lo", [P, KT, COLS], F32R)
        w_hi, w_lo = sb("w_hi", [P, RING, KT * P], F32R), sb("w_lo", [P, RING, KT * P], F32R)
        w_raw = sb("w_raw", [P, 2, KT * P])
        x_in = sb("x_in", [P, 2, D_MODEL])
        work = sb("work", [P, 2, 4 * 256])
        pt_hi, pt_lo = sb("pt_hi", [P, 1024], F32R), sb("pt_lo", [P, 1024], F32R)
        q_st = sb("q_st", [P, 4, COLS], F32R)
        kv_t = sb("kv_t", [P, WINDOW + COLS])
        k_hi, k_lo = sb("k_hi", [P, 2, K_COLS], F32R), sb("k_lo", [P, 2, K_COLS], F32R)
        v_st = sb("v_st", [P, 2, TILES + 3, P], F32R)
        silu_g = sb("silu_g", [P, 2, COLS])
        rstd_b = sb("rstd_b", [P, COLS])
        acc = sb("acc", [P, COLS])
        sq = sb("sq", [P, COLS])
        bias = sb("bias", [P, 4, 2 * WINDOW])
        dist = sb("dist", [P, 2 * WINDOW])
        kv_keep = sb("kv_keep", [P, GROUPS, WINDOW])
        kv_cache = sb("kv_cache", [P, GROUPS, P])
        u_keep, u_last = sb("u_keep", [P, KT, HIST]), sb("u_last", [P, KT, HIST])
        u_cache = sb("u_cache", [P, KT, HIST])
        nat = sb("nat", [P, P])
        ident, ones = sb("ident", [P, P]), sb("ones", [P, P])
        prm_rows, prm = sb("prm_rows", [P, P]), sb("prm", [P, R_ALL])
        c_t, c_s = sb("c_t", [P, 16]), sb("c_s", [P, 16])
        mod = sb("mod", [P, 2, 3 * KT, 2])
        gain = sb("gain", [P, 2, KT, 2])
        wb = sb("wb", [P, 2 * KT + 5 * GROUPS, 2])
        half_ps = sb("half_ps", [P, KT])
        inv_n = sb("inv_n", [P, GROUPS, HIST])
        ramp = sb("ramp", [P, HIST])
        head16 = sb("head16", [P, HIST])
        ss, var, rstd, power = sb("ss", [P, 5]), sb("var", [P, 5]), sb("rstd", [P, 5]), sb("power", [P, 5])
        sinks, neg_sink = sb("sinks", [P, HEADS]), sb("neg_sink", [P, HEADS])
        row_max, neg_max = sb("row_max", [P, 2, 4]), sb("neg_max", [P, 2, 4])
        row_sum, sink_arg, sink_exp = sb("row_sum", [P, 2, 4]), sb("sink_arg", [P, 2, 4]), sb("sink_exp", [P, 2, 4])
        denom, recip = sb("denom", [P, 2, 4]), sb("recip", [P, 2, 4])

        flat = work[:, :, :].rearrange("p a b -> p (a b)")
        u_rows = [flat[:, i * U_COLS:(i + 1) * U_COLS] for i in range(2)]
        win = flat[:, 2 * U_COLS:2 * U_COLS + S_COLS]
        diag = flat[:, 0:5 * P].rearrange("p (t c) -> p t c", t=5)
        h_hi, h_lo = h_all_hi[:, :, SHIFT:], h_all_lo[:, :, SHIFT:]
        og = acc[:, 0:256]
        bias_flat = bias[:, :, :].rearrange("p a b -> p (a b)")
        hist_rows, mod_rows = bias_flat[0:HIST - 1, :], bias_flat[0:2, :]
        offsets = kv_t[:, 0:2 * WINDOW]
        landing = [w_raw[:, 0, :], w_raw[:, 1, :], work[:, 0, :], work[:, 1, :], x_in[:, 0, :], x_in[:, 1, :]]
        c_pairs = c_s[:, :].rearrange("p (v k) -> p k v", v=2)
        h_half = sq[0:HEAD_DIM, 0:PART]

        ps_u = [ps(f"ps_u{i}", [P, 512]) for i in range(3)]
        ps_s, ps_t, ps_o = ps("ps_s", [P, 2, 512]), ps("ps_t", [P, 2, 512]), ps("ps_o", [P, 512])
        s_flat = ps_s[:, :, :].rearrange("p a b -> p (a b)")
        t_flat = ps_t[:, :, :].rearrange("p a b -> p (a b)")
        mod_bank = {0: (ps_u[0][:, :], ps_u[1][:, :]), 1: (ps_u[2][:, :], ps_o[:, :])}
        for m in range(2, 6):
            mod_bank[m] = (ps_s[:, 0, :], ps_s[:, 1, :])
        mod_turn = [ps_u[0] if m == 0 else ps_o for m in range(6)]

        const_loaded = sem("const_loaded")
        pool_const, dve_const = sem("pool_const"), sem("dve_const")
        prm_loaded = sem("prm_loaded")
        raw_loaded = [sem("raw_loaded0"), sem("raw_loaded1")]
        ada_loaded = [sem(f"ada_loaded{i}") for i in range(LANDING + 2)]
        mod_rows_ready, mod_turned, shift_ready = sem("mod_rows_ready"), sem("mod_turned"), sem("shift_ready")
        w_hi_ready, w_lo_ready, ada_done = sem("w_hi_ready"), sem("w_lo_ready"), sem("ada_done")
        prm_turned, prm_ready, c_tanh, c_ready, mod_ready = (
            sem("prm_turned"), sem("prm_ready"), sem("c_tanh"), sem("c_ready"), sem("mod_ready"))
        x_loaded = [sem("x_loaded0"), sem("x_loaded1")]
        x_turned, x_put_act, x_put_dve, x_squared = sem("x_turned"), sem("x_put_act"), sem("x_put_dve"), sem("x_squared")
        h_hi_ready, h_lo_ready = sem("h_hi_ready"), sem("h_lo_ready")
        ssum_done, var_ready, rstd_ready, diag_ready, rstd_spread, rb_ready = (
            sem("ssum_done"), sem("var_ready"), sem("rstd_ready"), sem("diag_ready"), sem("rstd_spread"), sem("rb_ready"))
        unit_done, scaled, biased, tanh_ready, gate_ready = (
            sem("unit_done"), sem("scaled"), sem("biased"), sem("tanh_ready"), sem("gate_ready"))
        pooled_ready, pooled_hi, pooled_lo = sem("pooled_ready"), sem("pooled_hi"), sem("pooled_lo")
        y_ready, yz_hi, yz_lo = sem("y_ready"), sem("yz_hi"), sem("yz_lo")
        x_new, sq_ready, acc_ready, x_scaled = sem("x_new"), sem("sq_ready"), sem("acc_ready"), sem("x_scaled")
        q_hi_ready, q_lo_ready = sem("q_hi_ready"), sem("q_lo_ready")
        k_prev, k_hi_half, k_lo_half, k_hi_ready, k_lo_ready = (
            sem("k_prev"), sem("k_hi_half"), sem("k_lo_half"), sem("k_hi_ready"), sem("k_lo_ready"))
        v_turned, v_hi_ready, v_lo_ready, kv_nat = (
            sem("v_turned"), sem("v_hi_ready"), sem("v_lo_ready"), sem("kv_nat"))
        bias_ready = sem("bias_ready")
        s_ready, max_ready, exp_ready, sink_ready, recip_ready, norm_ready = (
            sem("s_ready"), sem("max_ready"), sem("exp_ready"), sem("sink_ready"), sem("recip_ready"), sem("norm_ready"))
        p_turned, pt_hi_ready, pt_lo_ready, pv_done = (
            sem("p_turned"), sem("pt_hi_ready"), sem("pt_lo_ready"), sem("pv_done"))
        half_ready, og_ready, yo_hi, yo_lo = sem("half_ready"), sem("og_ready"), sem("yo_hi"), sem("yo_lo")
        state_turned, state_nat = sem("state_turned"), sem("state_nat")
        out_turned, out_act, out_dve = sem("out_turned"), sem("out_act"), sem("out_dve")
        nat_stored, cache_copied = sem("nat_stored"), sem("cache_copied")
        y_stored = [sem("y_stored0"), sem("y_stored1")]
        dve_chain, act_chain = sem("dve_chain"), sem("act_chain")

        def tile_used(eng, j):
            eng.wait_ge(unit_done, sched.last_unit[j] + 1)

        first = sched.first
        mod_at = {m: i + 1 for i, m in enumerate(sched.mods)}

        def ada_slot(i):
            return (i % LANDING, i // LANDING + 1) if i < first else (LANDING + i % 2, (i - first) // 2 + 1)

        def bank_of(u):
            return ps_u[u["u"] % 3][:, shifts(u):512]

        def shifts(u):
            return SHIFT if u["p"] == 0 and u["b"] == 0 and u["kind"] in ("u", "gate", "kv", "q", "agate") else 0

        loads, per_slot = [], [0, 0]
        for j, t in enumerate(tiles):
            per_slot[j % 2] += 32 if t[0] == "kv" else 16
            loads.append(per_slot[j % 2])
        width = [2 * 2 * P if t[0] == "grp" else KT * P for t in tiles]
        xt = [s for s in steps if s[0] == "XT"]
        xt_at = {s[1:]: n for n, s in enumerate(xt)}
        xt_act = {s[1:]: sum(1 for r in xt[:n + 1] if r[2] % 2 == 0) for n, s in enumerate(xt)}
        xt_dve = {s[1:]: sum(1 for r in xt[:n + 1] if r[2] % 2 == 1) for n, s in enumerate(xt)}
        ft = [s for s in steps if s[0] == "FT"]
        ft_at = {s[1:]: n for n, s in enumerate(ft)}
        ft_act = {s[1:]: sum(1 for r in ft[:n + 1] if r[2] % 2 == 0) for n, s in enumerate(ft)}
        ft_dve = {s[1:]: sum(1 for r in ft[:n + 1] if r[2] % 2 == 1) for n, s in enumerate(ft)}
        out_unit = {(u["p"], u["layer"], u["n"], u["b"]): u for u in units if u["kind"] == "out"}
        nat_order = [("state", 0)] + [("kv", 0, g) for g in range(GROUPS)] \
            + [("state", PARTS - 1)] + [("kv", PARTS - 1, g) for g in range(GROUPS)]
        nat_size = {k: 8 * 16 if k[0] == "state" else 2 * 16 for k in nat_order}

        def nat_free(eng, key):
            before = sum(nat_size[k] for k in nat_order[:nat_order.index(key)])
            if before:
                eng.wait_ge(nat_stored, before)

        def norms(p, r):
            return 3 * p + r + 1

        def cols(p):
            return COLS if p == 0 else PART

        def tok_span(t):
            return (COLS - P, P - SAMPLE) if t == TILES else (t * P, 0)

        def item_blocks(it):
            out = []
            for n, t in enumerate(it["tiles"]):
                for e in range(2):
                    out.append((2 * n + e, t, e, WINDOW if (it["p"] == 0 and t == 0) else 0))
            return out

        def span_of(it):
            if it["sample"]:
                return 0, 4 * SAMPLE
            return (256 if (it["p"] == 0 and it["tiles"][0] == 0) else 0), 1024

        block = ctx.enter_context(nc.Block())

        @block.sync
        def _(sp):
            def load_tile(j):
                t = tiles[j]
                dst = w_raw[:, j % 2, :].rearrange("p (k n) -> p k n", k=KT)
                if j >= 2:
                    sp.wait_ge(w_hi_ready, j - 1)
                    sp.wait_ge(w_lo_ready, j - 1)
                else:
                    sp.wait_ge(ada_done, first - LANDING + j + 1)
                s = raw_loaded[j % 2]
                if t[0] == "pin":
                    sp.dma_start(dst, I["pool_w_in"][0].rearrange("(k p) n -> p k n", p=P)[:, :, t[1] * P:(t[1] + 1) * P]).then_inc(s, 16)
                elif t[0] == "grp":
                    sp.dma_start(w_raw[:, j % 2, 0:4 * P].rearrange("p (k n) -> p k n", k=2),
                                 I["pool_w_grp"][0, t[1]].rearrange("(k p) n -> p k n", p=P)).then_inc(s, 16)
                elif t[0] == "pout":
                    sp.dma_start(dst, I["pool_w_out"][0].rearrange("(k p) n -> p k n", p=P)[:, :, t[1] * P:(t[1] + 1) * P]).then_inc(s, 16)
                elif t[0] == "aout":
                    sp.dma_start(dst, I["attn_w_out"][0].rearrange("(k p) n -> p k n", p=P)[:, :, t[1] * P:(t[1] + 1) * P]).then_inc(s, 16)
                elif t[0] == "ain":
                    sp.dma_start(dst, I["attn_w_in"][0].rearrange("(k p) n -> p k n", p=P)[:, :, t[1]:t[1] + P]).then_inc(s, 16)
                else:
                    src = I["attn_w_in"][0].rearrange("(k p) n -> p k n", p=P)
                    for half, at in enumerate((1024, 1280)):
                        sp.dma_start(dst[:, :, half * 64:half * 64 + 64],
                                     src[:, :, at + 64 * t[1]:at + 64 * t[1] + 64]).then_inc(s, 16)

            def load_ada(i):
                l, what = sched.mods[i // KT]
                half, pair = divmod(i % KT, 4)
                slot, nth = ada_slot(i)
                if i >= first:
                    sp.wait_ge(x_squared, TILES + 1)
                    if i >= first + 2:
                        sp.wait_ge(ada_done, i - 1)
                elif i >= LANDING:
                    sp.wait_ge(ada_done, i - LANDING + 1)
                at = what * D_MODEL + half * 512
                sp.dma_start(landing[slot].rearrange("p (k n) -> p k n", k=2),
                             I["ada_w"][l].rearrange("(k p) n -> p k n", p=P)[:, 2 * pair:2 * pair + 2, at:at + 512]).then_inc(ada_loaded[slot], 16)

            for name, at in (("ada_b", R_ADA_B), ("norm_g", R_NORM), ("final_g", R_FINAL), ("pool_scale", R_POOL),
                             ("c_prompt", R_C), ("c_sample", R_C + KT)):
                a = I[name] if name != "final_g" else I[name].rearrange("(o n) -> o n", o=1)
                rows = a.rearrange("l (k p) -> (l k) p", p=P)
                sp.dma_start(prm_rows[at:at + rows.shape[0], :], rows).then_inc(prm_loaded, 16)
            for i in range(LANDING):
                load_ada(i)
            sp.dma_start(hist_rows, I["cache_pool"][0, 0]).then_inc(const_loaded, 16)
            sp.dma_start(sinks[:, :], I["attn_sinks"].to_broadcast([P, HEADS])).then_inc(const_loaded, 16)
            sp.dma_start(kv_cache[:, :, 0:64], I["cache_k"][0, 0]).then_inc(const_loaded, 16)
            sp.dma_start(kv_cache[:, :, 64:128], I["cache_v"][0, 0]).then_inc(const_loaded, 16)
            sp.dma_start(O[6][0, 0, 0:WINDOW - SAMPLE], I["cache_k"][0, 0, SAMPLE:WINDOW]).then_inc(cache_copied, 16)
            sp.dma_start(O[7][0, 0, 0:WINDOW - SAMPLE], I["cache_v"][0, 0, SAMPLE:WINDOW]).then_inc(cache_copied, 16)
            for st in steps:
                if st[0] == "ADA":
                    i = st[1]
                    if i < first - LANDING:
                        load_ada(i + LANDING)
                    elif i < first - 2:
                        load_tile(i - first + LANDING)
                    elif i + 2 < KT * len(sched.mods):
                        load_ada(i + 2)
                elif st[0] == "W" and st[1] + 2 < len(tiles):
                    load_tile(st[1] + 2)
                elif st[0] == "XL":
                    _, p, t = st
                    n = xt_at[(p, t)]
                    if p == 1:
                        sp.wait_ge(ada_done, KT * len(sched.mods))
                    if n >= 2:
                        sp.wait_ge(x_squared, n - 1)
                    if t == TILES:
                        sp.dma_start(x_in[P - SAMPLE:P, n % 2, :], I["x_sample"][0]).then_inc(x_loaded[n % 2], 16)
                    else:
                        r0 = p * PART + t * P
                        sp.dma_start(x_in[:, n % 2, :], I["x_prompt"][0, r0:r0 + P, :]).then_inc(x_loaded[n % 2], 16)
            sp.wait_ge(cache_copied, 32)

        @block.tensor
        def _(pe):
            free = {"s": [], "t": [], "o": []}

            def claim(bank, *readers):
                for s, v in free[bank]:
                    pe.wait_ge(s, v)
                free[bank] = list(readers)

            def split_product(out, pairs):
                n = 3 * len(pairs)
                i = 0
                for whi, wlo, xhi, xlo in pairs:
                    for w, x in ((whi, xhi), (whi, xlo), (wlo, xhi)):
                        last = nc.tensor.matmul(out, w, x, start=(i == 0), stop=(i == n - 1))
                        i += 1
                return last

            pe.wait_ge(prm_loaded, 6 * 16)
            pe.wait_ge(pool_const, 2)
            claim("t", (prm_ready, 1))
            nc.tensor.transpose(t_flat[:, 0:R_ALL], prm_rows[0:R_ALL, :], ident[0:R_ALL, 0:R_ALL]).then_inc(prm_turned, 1)
            pe.wait_ge(const_loaded, 4 * 16)
            claim("s", (prm_ready, 2))
            for k in range(KT):
                last = nc.tensor.transpose(s_flat[:, k * HIST:k * HIST + HIST - 1], hist_rows[:, k * P:(k + 1) * P],
                                           ident[0:HIST - 1, 0:HIST - 1])
            last.then_inc(prm_turned, 1)
            pe.wait_ge(dve_const, 1)
            pe.wait_ge(c_ready, 1)

            for st in steps:
                kind = st[0]
                if kind == "ADA":
                    i = st[1]
                    m, half, pair = i // KT, i % KT // 4, i % 4
                    if m == 1 and i % KT == 0:
                        claim("o", (mod_ready, 2))
                    if m >= 2 and i % KT == 0:
                        claim("s", (mod_rows_ready, m + 1))
                    slot, nth = ada_slot(i)
                    pe.wait_ge(ada_loaded[slot], 16 * nth)
                    for k in range(2):
                        last = nc.tensor.matmul(mod_bank[m][half][0:2, :], c_pairs[:, 2 * pair + k, :],
                                                landing[slot][:, 512 * k:512 * (k + 1)],
                                                start=(pair == 0 and k == 0), stop=(pair == 3 and k == 1))
                    last.then_inc(ada_done, 1)
                elif kind == "MT":
                    m = st[1]
                    if m >= 2:
                        claim("o", (mod_ready, m + 1))
                    pe.wait_ge(mod_rows_ready, m + 1)
                    for k in range(KT):
                        last = nc.tensor.transpose(mod_turn[m][:, 2 * k:2 * k + 2], mod_rows[:, k * P:(k + 1) * P], ident[0:2, 0:2])
                    last.then_inc(mod_turned, 1)
                elif kind == "XT":
                    _, p, t = st
                    n = xt_at[(p, t)]
                    pe.wait_ge(x_loaded[n % 2], 16 * (n // 2 + 1))
                    _, r0 = tok_span(t)
                    if t % 2 == 0:
                        claim("s", (x_put_act, xt_act[(p, t)]))
                    else:
                        claim("t", (x_put_dve, xt_dve[(p, t)]))
                    bank = (s_flat, t_flat)[t % 2]
                    for k in range(KT):
                        last = nc.tensor.transpose(bank[:, k * P:(k + 1) * P - r0], x_in[r0:P, n % 2, k * P:(k + 1) * P],
                                                   ident[r0:P, r0:P])
                    last.then_inc(x_turned, 1)
                elif kind == "NA" and st[2] > 0:
                    _, p, r = st
                    claim("o", (var_ready, norms(p, r)))
                    pe.wait_ge(acc_ready, (2 * p + r) * KT)
                    for t in range(TILES + (p == 0)):
                        c0, _ = tok_span(t)
                        last = nc.tensor.matmul(ps_o[:, t:t + 1], acc[:, c0:c0 + P], ones[:, 0:1], start=True, stop=True)
                    last.then_inc(ssum_done, 1)
                elif kind == "NB":
                    _, p, r = st
                    claim("t", (rb_ready, 2 * p + r + 1))
                    pe.wait_ge(diag_ready, 2 * p + r + 1)
                    last = nc.tensor.matmul(ps_t[:, 0, :], ones[:, :], flat[:, 0:PART], start=True, stop=True)
                    if p == 0:
                        last = nc.tensor.matmul(ps_t[:, 1, 0:SAMPLE], ones[:, :], diag[:, TILES, P - SAMPLE:P],
                                                start=True, stop=True)
                    last.then_inc(rstd_spread, 1)
                elif kind == "U":
                    u = units[st[1]]
                    p, j, c0, w = u["p"], u["j"], u["c0"], u["w"]
                    if u["u"] == 0:
                        pe.wait_ge(mod_ready, 1)
                    if u["u"] in (1, 2):
                        pe.wait_ge(mod_rows_ready, u["u"])
                    if u["u"] >= 3:
                        v = units[u["u"] - 3]
                        if v["kind"] in ("u", "kv"):
                            pe.wait_ge(biased, v["nth_proj"])
                        elif v["kind"] in ("gate", "agate"):
                            pe.wait_ge(gate_ready, v["nth_anygate"])
                        elif v["kind"] == "q":
                            pe.wait_ge(q_lo_ready, v["nth_q"])
                        elif v["kind"] == "z":
                            pe.wait_ge(y_ready, v["nth_z"])
                        else:
                            pe.wait_ge(x_new, v["nth_out"])
                    pe.wait_ge(w_hi_ready, j + 1)
                    pe.wait_ge(w_lo_ready, j + 1)
                    bank = ps_u[u["u"] % 3]
                    slot = j % RING
                    if u["kind"] == "z":
                        pe.wait_ge(pooled_hi, 8 * p + 2 * u["g"] + 2)
                        pe.wait_ge(pooled_lo, 8 * p + 2 * u["g"] + 2)
                        at = [2 * P * k + P * u["m"] for k in range(2)]
                        last = split_product(bank[:, 0:w], [
                            (w_hi[:, slot, a:a + P], w_lo[:, slot, a:a + P], q_st[:, k, c0:c0 + w], q_st[:, 2 + k, c0:c0 + w])
                            for k, a in enumerate(at)])
                    else:
                        if u["kind"] == "out":
                            if u["layer"] == 0:
                                n = sum(1 for x in units if x["kind"] == "z" and x["p"] <= p)
                                pe.wait_ge(yz_hi, n)
                                pe.wait_ge(yz_lo, n)
                            else:
                                n = sum(1 for x in items if x["p"] <= p)
                                pe.wait_ge(yo_hi, n)
                                pe.wait_ge(yo_lo, n)
                            xh, xl = y_hi, y_lo
                        else:
                            n = 16 * p + (8 if u["kind"] in ("u", "gate") else 16)
                            pe.wait_ge(h_hi_ready, n)
                            pe.wait_ge(h_lo_ready, n)
                            xh, xl = h_all_hi, h_all_lo
                            c0, w = c0 + SHIFT - shifts(u), w + shifts(u)
                            if shifts(u):
                                pe.wait_ge(shift_ready, 1 if u["kind"] in ("u", "gate") else 2)
                        last = split_product(bank[:, 0:w], [
                            (w_hi[:, slot, k * P:(k + 1) * P], w_lo[:, slot, k * P:(k + 1) * P],
                             xh[:, k, c0:c0 + w], xl[:, k, c0:c0 + w]) for k in range(KT)])
                    last.then_inc(unit_done, 1)
                elif kind == "PS":
                    p = st[1]
                    claim("o", (state_nat, 1 if p == 0 else 2))
                    pe.wait_ge(pooled_ready, 8 * p + 8)
                    src = u_last if p == 0 else u_keep
                    nc.tensor.transpose(ps_o[:, 0:P], src[:, :, :].rearrange("p k c -> p (k c)"), ident[:, :]).then_inc(state_turned, 1)
                elif kind == "VT":
                    _, p, g = st
                    n = GROUPS * p + g + 1
                    claim("t", (v_lo_ready, n))
                    pe.wait_ge(biased, next(u["nth_proj"] for u in reversed(units)
                                            if u["kind"] == "kv" and u["p"] == p and u["g"] == g))
                    pe.wait_ge(k_prev, n)
                    first = 0 if p else 1
                    for b in range(TILES + 1 - first):
                        last = nc.tensor.transpose(t_flat[:, b * P:(b + 1) * P], kv_t[:, (first + b) * P:(first + b + 1) * P], ident[:, :])
                    if p == 0:
                        nc.tensor.transpose(t_flat[:, 4 * P:5 * P], kv_cache[:, g, :], ident[:, :])
                        last = nc.tensor.transpose(t_flat[:, 5 * P:6 * P], kv_t[:, COLS:COLS + P], ident[:, :])
                    last.then_inc(v_turned, 1)
                elif kind == "S":
                    it = items[st[1]]
                    a, p, g, d = it["a"], it["p"], it["g"], it["g"] % 2
                    claim("s", (max_ready, a + 1))
                    n = GROUPS * p + g + 1
                    pe.wait_ge(k_hi_ready, n)
                    pe.wait_ge(k_lo_ready, n)
                    qn = max(u["nth_q"] for u in units if u["kind"] == "q" and u["p"] == p and u["g"] == g and u["i"] == it["hp"])
                    pe.wait_ge(q_hi_ready, qn)
                    pe.wait_ge(q_lo_ready, qn)
                    for at, t, e, k0 in item_blocks(it):
                        c0, _ = tok_span(t)
                        if it["sample"]:
                            out, kc = s_flat[:, at * 256:at * 256 + WINDOW + SAMPLE], slice(K_CACHE, K_COLS)
                        else:
                            out, kc = s_flat[:, at * 256 + k0:at * 256 + 256], slice(t * P + k0, t * P + 256)
                        q = q_st[:, 2 * it["hp"] + e, c0:c0 + P]
                        nc.tensor.matmul(out, q, k_hi[:, d, kc], start=True, stop=False)
                        last = nc.tensor.matmul(out, q, k_lo[:, d, kc], start=False, stop=True)
                    last.then_inc(s_ready, 1)
                elif kind == "TR":
                    it = items[st[1]]
                    a = it["a"]
                    claim("t", (pt_lo_ready, a + 1))
                    pe.wait_ge(norm_ready, a + 1)
                    for at, t, e, k0 in item_blocks(it):
                        if it["sample"]:
                            r = slice(P - SAMPLE, P)
                            for kt in range(2):
                                o = (2 * kt + e) * SAMPLE
                                src = work[r, a % 2, at * 256 + kt * SAMPLE:at * 256 + kt * SAMPLE + P]
                                last = nc.tensor.transpose(t_flat[:, o:o + SAMPLE], src, ident[r, r])
                        else:
                            for kt in range(k0 // P, 2):
                                o = (4 * (at // 2) + 2 * kt + e) * P
                                last = nc.tensor.transpose(t_flat[:, o:o + P], work[:, a % 2, at * 256 + kt * P:at * 256 + (kt + 1) * P],
                                                           ident[:, :])
                    last.then_inc(p_turned, 1)
                elif kind == "PV":
                    it = items[st[1]]
                    a, p, g, d = it["a"], it["p"], it["g"], it["g"] % 2
                    claim("o", (og_ready, a + 1))
                    pe.wait_ge(pt_hi_ready, a + 1)
                    pe.wait_ge(pt_lo_ready, a + 1)
                    pe.wait_ge(v_hi_ready, GROUPS * p + g + 1)
                    pe.wait_ge(v_lo_ready, GROUPS * p + g + 1)
                    if it["sample"]:
                        r = slice(P - SAMPLE, P)
                        mms = [(v_st[:, d, TILES + 1, :], slice(0, P), 0), (v_st[r, d, TILES + 2, :], r, 64)]
                        i = 0
                        for v, rr, o in mms:
                            for pt in (pt_hi, pt_lo):
                                last = nc.tensor.matmul(ps_o[:, 0:64], v, pt[rr, o:o + 64], start=(i == 0), stop=(i == 3))
                                i += 1
                    else:
                        for n, t in enumerate(it["tiles"]):
                            kts = (1,) if (p == 0 and t == 0) else (0, 1)
                            i = 0
                            for kt in kts:
                                o = (4 * n + 2 * kt) * P
                                for pt in (pt_hi, pt_lo):
                                    last = nc.tensor.matmul(ps_o[:, n * 256:n * 256 + 256], v_st[:, d, t + kt, :], pt[:, o:o + 256],
                                                            start=(i == 0), stop=(i == 2 * len(kts) - 1))
                                    i += 1
                    last.then_inc(pv_done, 1)
                elif kind == "FT":
                    _, p, t = st
                    n = ft_at[(p, t)]
                    if t % 2 == 0:
                        claim("s", (out_act, ft_act[(p, t)]))
                    else:
                        claim("t", (out_dve, ft_dve[(p, t)]))
                    bank = (s_flat, t_flat)[t % 2]
                    pe.wait_ge(x_scaled, (p + 1) * KT)
                    c0, _ = tok_span(t)
                    for k in range(KT):
                        last = nc.tensor.transpose(bank[:, k * P:(k + 1) * P], x_res[:, k, c0:c0 + P], ident[:, :])
                    last.then_inc(out_turned, 1)

        @block.vector
        def _(dve):
            n_chain = [0]

            def link(ins):
                n_chain[0] += 1
                ins.then_inc(dve_chain, 1)
                dve.wait_ge(dve_chain, n_chain[0])

            V = nc.vector
            V.memset(ones[:, :], 1.0)
            V.memset(power[:, :], -0.5)
            V.memset(u_keep[:, :, :], 0.0)
            V.memset(u_cache[:, :, :], 0.0)
            V.memset(ss[:, :], 1.0).then_inc(dve_const, 1)
            for t in range(HIST):
                last = V.memset(ramp[:, t:t + 1], float(t + 1))
            link(last)
            for g in range(GROUPS):
                last = V.tensor_scalar(inv_n[:, g, :], ramp[:, :], float(WINDOWS[g]), None, ALU.min)
            link(last)
            link(V.reciprocal(inv_n[:, :, :], inv_n[:, :, :]))
            dve.wait_ge(pool_const, 3)
            link(V.tensor_copy(dist[:, :], offsets.bitcast(I32)))
            link(V.scalar_tensor_tensor(out=dist[:, :], in0=dist[:, :], scalar=-1.0, in1=dist[:, :], op0=ALU.mult, op1=ALU.max))
            V.memset(dist[0:64, 192:256], BIG)
            V.memset(dist[64:128, 0:64], BIG).then_inc(dve_const, 1)
            dve.wait_ge(const_loaded, 4 * 16)
            link(V.tensor_scalar(neg_sink[:, :], sinks[:, :], -1.0, None, ALU.mult))
            dve.wait_ge(c_tanh, 1)
            link(V.scalar_tensor_tensor(out=c_s[:, :], in0=c_t[:, :], scalar=1.0, in1=prm[:, R_C:R_C + 16], op0=ALU.add, op1=ALU.mult))
            V.tensor_scalar(c_s[:, :], c_s[:, :], 0.5, None, ALU.mult).then_inc(c_ready, 1)
            link(V.tensor_scalar(half_ps[:, :], prm[:, R_POOL:R_POOL + KT], 0.5, None, ALU.mult))
            dve.wait_ge(prm_turned, 2)
            V.tensor_copy(u_cache[:, :, 1:HIST], s_flat[:, 0:KT * HIST].rearrange("p (k c) -> p k c", k=KT)[:, :, 0:HIST - 1]).then_inc(prm_ready, 1)

            for st in steps:
                kind = st[0]
                if kind == "MT":
                    m = st[1]
                    l, what = sched.mods[m]
                    ns = slice(KT * what, KT * (what + 1))
                    dve.wait_ge(mod_turned, m + 1)
                    add = V.tensor_tensor(mod[:, l, ns, :], mod_turn[m][:, 0:2 * KT].rearrange("p (n v) -> p n v", v=2),
                                          prm[:, R_ADA_B + 24 * l + KT * what:R_ADA_B + 24 * l + KT * (what + 1)]
                                          .unsqueeze(2).to_broadcast([P, KT, 2]), ALU.add)
                    if what == 1:
                        link(add)
                        add = V.scalar_tensor_tensor(out=gain[:, l], in0=mod[:, l, ns, :], scalar=1.0,
                                                     in1=prm[:, R_NORM + KT * l:R_NORM + KT * (l + 1)].unsqueeze(2).to_broadcast([P, KT, 2]),
                                                     op0=ALU.add, op1=ALU.mult)
                    add.then_inc(mod_ready, 1)
                    dve.wait_ge(mod_ready, m + 1)
                elif kind == "SH":
                    l = st[1]
                    if l:
                        dve.wait_ge(unit_done, 1 + next(u["u"] for u in reversed(units) if u["kind"] == "gate" and u["p"] == 0))
                    link(V.tensor_copy(h_all_hi[:, :, 0:SHIFT], mod[:, l, 0:KT, :]))
                    V.tensor_tensor(h_all_lo[:, :, 0:SHIFT], mod[:, l, 0:KT, :], h_all_hi[:, :, 0:SHIFT].bitcast(F32),
                                    ALU.subtract).then_inc(shift_ready, 1)
                elif kind == "XT":
                    _, p, t = st
                    if t % 2 == 1:
                        dve.wait_ge(x_turned, xt_at[(p, t)] + 1)
                        if p:
                            dve.wait_ge(out_turned, ft_at[(p - 1, TILES - 1)] + 1 + (p == 1))
                        V.tensor_copy(x_res[:, :, t * P:(t + 1) * P], t_flat.rearrange("p (k c) -> p k c", k=KT)).then_inc(x_put_dve, 1)
                elif kind == "HS":
                    _, p, k = st
                    dve.wait_ge(h_hi_ready, 16 * p + k + 1)
                    if k == 0:
                        dve.wait_ge(x_put_dve, xt_dve[(p, TILES - 1)])
                        dve.wait_ge(x_put_act, xt_act[(p, TILES if p == 0 else TILES - 2)])
                    for c, w, v in spans(0, cols(p)):
                        last = V.scalar_tensor_tensor(out=h_lo[:, k, c:c + w], in0=x_res[:, k, c:c + w], scalar=gain[:, 0, k, v:v + 1],
                                                      in1=h_hi[:, k, c:c + w].bitcast(F32), op0=ALU.mult, op1=ALU.subtract)
                    last.then_inc(h_lo_ready, 1)
                elif kind == "NA":
                    _, p, r = st
                    nt = TILES + (p == 0)
                    if r == 0:
                        dve.wait_ge(x_squared, xt_at[(p, nt - 1)] + 1)
                        src = ss[:, 0:nt]
                    else:
                        dve.wait_ge(ssum_done, 2 * p + r)
                        src = ps_o[:, 0:nt]
                    if 3 * p + r:
                        dve.wait_ge(rstd_ready, norms(p, r) - 1)
                    V.tensor_scalar(var[:, 0:nt], src, 1.0 / D_MODEL, EPS, ALU.mult, ALU.add).then_inc(var_ready, 1)
                    if r < 2:
                        dve.wait_ge(rstd_ready, norms(p, r))
                        if r:
                            dve.wait_ge(unit_done, next(u["u"] for u in reversed(units) if u["kind"] == "z" and u["p"] == p))
                        elif p:
                            n_items = sum(1 for x in items if x["p"] < p)
                            dve.wait_ge(p_turned, n_items)
                            dve.wait_ge(y_stored[0], 16 * ((ft_at[(p - 1, TILES - 1 + (p == 1))]) // 2 + 1))
                            dve.wait_ge(y_stored[1], 16 * ((ft_at[(p - 1, TILES - 1 + (p == 1))] + 1) // 2))
                        V.tensor_tensor(diag[:, 0:nt, :], ident[:, :].unsqueeze(1).to_broadcast([P, nt, P]),
                                        rstd[:, 0:nt].unsqueeze(2).to_broadcast([P, nt, P]), ALU.mult).then_inc(diag_ready, 1)
                elif kind == "E1":
                    u = units[st[1]]
                    p, c0, w, k = u["p"], u["c0"], u["w"], u["kind"]
                    bank = bank_of(u)
                    dve.wait_ge(unit_done, u["u"] + 1)
                    if k in ("u", "gate", "kv", "q", "agate"):
                        if p == 0 and u["b"] == 0:
                            V.tensor_copy(wb[:, u["n"], :], ps_u[u["u"] % 3][:, 0:SHIFT])
                        dve.wait_ge(rb_ready, 2 * p + (1 if k in ("u", "gate") else 2))
                        V.tensor_tensor(bank[:, 0:w], bank[:, 0:w], rstd_b[:, c0:c0 + w], ALU.mult).then_inc(scaled, 1)
                    elif k == "z":
                        i = u["m"]
                        gates = [x for x in units if x["kind"] == "gate" and x["p"] == p and x["g"] == u["g"] and x["i"] == i and x["b"] == u["b"]]
                        dve.wait_ge(gate_ready, gates[0]["nth_anygate"])
                        if u["nth_z"] > 1:
                            dve.wait_ge(yz_hi, u["nth_z"] - 1)
                            dve.wait_ge(yz_lo, u["nth_z"] - 1)
                        if p:
                            dve.wait_ge(yo_hi, sum(1 for x in items if x["p"] < p))
                            dve.wait_ge(yo_lo, sum(1 for x in items if x["p"] < p))
                        V.scalar_tensor_tensor(out=acc[:, c0:c0 + w], in0=bank[:, 0:w], scalar=half_ps[:, u["n"]:u["n"] + 1],
                                               in1=silu_g[:, i, c0:c0 + w], op0=ALU.mult, op1=ALU.mult).then_inc(y_ready, 1)
                        dve.wait_ge(yz_hi, u["nth_z"])
                        dve.wait_ge(y_ready, u["nth_z"])
                        V.tensor_tensor(y_lo[:, u["n"], c0:c0 + w], acc[:, c0:c0 + w], y_hi[:, u["n"], c0:c0 + w].bitcast(F32),
                                        ALU.subtract).then_inc(yz_lo, 1)
                    else:
                        l, n = u["layer"], u["n"]
                        for c, ww, v in spans(c0, w):
                            last = V.scalar_tensor_tensor(out=x_res[:, n, c:c + ww], in0=bank[:, c - c0:c - c0 + ww],
                                                          scalar=mod[:, l, 2 * KT + n, v:v + 1], in1=x_res[:, n, c:c + ww],
                                                          op0=ALU.mult, op1=ALU.add)
                        last.then_inc(x_new, 1)
                elif kind == "E2":
                    u = units[st[1]]
                    p, c0, w, k = u["p"], u["c0"], u["w"], u["kind"]
                    bank = bank_of(u)
                    if k in ("gate", "agate"):
                        dve.wait_ge(tanh_ready, u["nth_anygate"])
                        V.scalar_tensor_tensor(out=silu_g[:, u["i"], c0:c0 + w], in0=silu_g[:, u["i"], c0:c0 + w], scalar=1.0,
                                               in1=bank[:, 0:w], op0=ALU.add, op1=ALU.mult).then_inc(gate_ready, 1)
                    elif k == "q":
                        dve.wait_ge(q_hi_ready, u["nth_q"])
                        for e in range(2):
                            q = q_st[:, 2 * u["i"] + e, c0:c0 + w]
                            last = V.tensor_tensor(q[64:128], bank[64 * e:64 * e + 64, 0:w], q[0:64].bitcast(F32), ALU.subtract)
                        last.then_inc(q_lo_ready, 1)
                    else:
                        n = u["n"]
                        if u["b"] == len(sched.blocks(p)) - 1:
                            dve.wait_ge(h_hi_ready, 16 * p + 8 + n + 1)
                            for c, ww, v in spans(0, cols(p)):
                                last = V.scalar_tensor_tensor(out=h_lo[:, n, c:c + ww], in0=x_res[:, n, c:c + ww],
                                                              scalar=gain[:, 1, n, v:v + 1], in1=h_hi[:, n, c:c + ww].bitcast(F32),
                                                              op0=ALU.mult, op1=ALU.subtract)
                            last.then_inc(h_lo_ready, 1)
                elif kind == "PL":
                    _, p, g, i = st
                    n = 8 * p + 2 * g + i
                    row, wdw = u_rows[i], WINDOWS[g]
                    dve.wait_ge(biased, next(x["nth_proj"] for x in reversed(units)
                                             if x["kind"] == "u" and x["p"] == p and x["g"] == g and x["i"] == i))
                    V.memset(row[:, 0:HIST], 0.0)
                    link(V.tensor_copy(row[:, HIST:2 * HIST], u_keep[:, 2 * g + i, :]))
                    if p == 0:
                        V.memset(row[:, U_PROMPT + PART:U_PROMPT + PART + HIST], 0.0)
                        link(V.tensor_copy(row[:, U_SAMPLE - HIST:U_SAMPLE], u_cache[:, 2 * g + i, :]))
                        V.tensor_copy(u_last[:, 2 * g + i, :], row[:, U_COLS - HIST:U_COLS])
                    V.tensor_copy(u_keep[:, 2 * g + i, :], row[:, U_PROMPT + PART - HIST:U_PROMPT + PART])
                    last = V.tensor_tensor_scan(win[:, 0:HIST + PART], row[:, HIST:U_PROMPT + PART],
                                                row[:, HIST - wdw:U_PROMPT + PART - wdw], 0.0, ALU.add, ALU.subtract)
                    if p == 0:
                        last = V.tensor_tensor_scan(win[:, HIST + PART:S_COLS], row[:, U_SAMPLE - HIST:U_COLS],
                                                    row[:, U_SAMPLE - HIST - wdw:U_COLS - wdw], 0.0, ALU.add, ALU.subtract)
                    link(last)
                    if n:
                        dve.wait_ge(pooled_hi, n)
                        dve.wait_ge(pooled_lo, n)
                    if p:
                        dve.wait_ge(acc_ready, 2 * p * KT)
                    first = 0
                    if p == 0:
                        first = HIST
                        link(V.tensor_tensor(head16[:, :], win[:, HIST:2 * HIST], inv_n[:, g, :], ALU.mult))
                        V.tensor_tensor(sq[:, 0:HIST], head16[:, :], row[:, U_PROMPT:U_PROMPT + HIST], ALU.subtract)
                        V.scalar_tensor_tensor(out=sq[:, PART:COLS], in0=win[:, 2 * HIST + PART:S_COLS], scalar=1.0 / wdw,
                                               in1=row[:, U_SAMPLE:U_COLS], op0=ALU.mult, op1=ALU.subtract)
                    V.scalar_tensor_tensor(out=sq[:, first:PART], in0=win[:, HIST + first:HIST + PART], scalar=1.0 / wdw,
                                           in1=row[:, U_PROMPT + first:U_PROMPT + PART], op0=ALU.mult, op1=ALU.subtract).then_inc(pooled_ready, 1)
                    dve.wait_ge(pooled_ready, n + 1)
                    dve.wait_ge(pooled_hi, n + 1)
                    V.tensor_tensor(q_st[:, 2 + i, 0:cols(p)], sq[:, 0:cols(p)], q_st[:, i, 0:cols(p)].bitcast(F32),
                                    ALU.subtract).then_inc(pooled_lo, 1)
                elif kind == "KS":
                    _, p, g = st
                    d, n = g % 2, GROUPS * p + g + 1
                    dve.wait_ge(biased, next(u["nth_proj"] for u in reversed(units)
                                             if u["kind"] == "kv" and u["p"] == p and u["g"] == g))
                    if n > 1:
                        dve.wait_ge(v_turned, n - 1)
                        dve.wait_ge(k_hi_half, n - 1)
                        dve.wait_ge(k_lo_half, n - 1)
                    if p:
                        link(V.tensor_copy(kv_t[:, 0:WINDOW], kv_keep[:, g, :]))
                    V.tensor_copy(kv_keep[:, g, :], kv_t[:, PART:PART + WINDOW]).then_inc(k_prev, 1)
                    dve.wait_ge(k_prev, n)
                    dve.wait_ge(k_hi_half, n)
                    a = 0 if p else WINDOW
                    last = V.tensor_tensor(k_lo[0:64, d, a:K_CACHE], kv_t[0:64, a:K_CACHE], k_hi[0:64, d, a:K_CACHE].bitcast(F32), ALU.subtract)
                    if p == 0:
                        last = V.tensor_tensor(k_lo[0:64, d, K_NEW:K_COLS], kv_t[0:64, K_CACHE:K_CACHE + SAMPLE],
                                               k_hi[0:64, d, K_NEW:K_COLS].bitcast(F32), ALU.subtract)
                    last.then_inc(k_lo_half, 1)
                elif kind == "VT":
                    _, p, g = st
                    d, n = g % 2, GROUPS * p + g + 1
                    dve.wait_ge(v_hi_ready, n)
                    dve.wait_ge(v_turned, n)
                    src = t_flat.rearrange("p (b c) -> p b c", c=P)
                    a = 0 if p else 1
                    m = TILES + 1 - a
                    last = V.tensor_tensor(v_st[:, d, a:TILES + 1, 64:128], src[:, 0:m, 64:128],
                                           v_st[:, d, a:TILES + 1, 0:64].bitcast(F32), ALU.subtract)
                    r = slice(P - SAMPLE, P)
                    if p == 0:
                        V.tensor_tensor(v_st[r, d, TILES + 2, 64:128], src[r, 5, 64:128], v_st[r, d, TILES + 2, 0:64].bitcast(F32), ALU.subtract)
                        V.tensor_tensor(v_st[:, d, TILES + 1, 64:128], kv_cache[:, g, 64:128], v_st[:, d, TILES + 1, 0:64].bitcast(F32), ALU.subtract)
                        last = V.tensor_tensor(k_lo[0:64, d, K_CACHE:K_NEW], src[0:64, 4, :], k_hi[0:64, d, K_CACHE:K_NEW].bitcast(F32), ALU.subtract)
                    if p in (0, PARTS - 1):
                        nat_free(dve, ("kv", p, g))
                        if g == 0:
                            dve.wait_ge(state_nat, 1 if p == 0 else 2)
                        rows, b = (r, 5) if p == 0 else (slice(0, P), TILES)
                        V.tensor_copy(nat[rows, :], src[rows, b, :]).then_inc(kv_nat, 1)
                        dve.wait_ge(kv_nat, g + 1 + (4 if p else 0))
                    link(last)
                    a, e = (0, K_CACHE) if p else (WINDOW, K_COLS)
                    V.tensor_copy(k_lo[64:128, d, a:e], k_lo[0:64, d, a:e].bitcast(F32)).then_inc(k_lo_ready, 1)
                    link(V.tensor_copy(head16[:, 0:1], ones[:, 0:1]))
                    V.tensor_copy(head16[:, 1:2], ones[:, 0:1]).then_inc(v_lo_ready, 1)
                elif kind == "SM":
                    it = items[st[1]]
                    a, g, hp = it["a"], it["g"], it["hp"]
                    d = a % 2
                    nb = 2 * len(it["tiles"])
                    r = slice(P - SAMPLE, P) if it["sample"] else slice(0, P)
                    dve.wait_ge(s_ready, a + 1)
                    dve.wait_ge(bias_ready, 8 * it["p"] + 2 * g + hp + 1)
                    if a >= 2:
                        dve.wait_ge(p_turned, a - 1)
                    for at, t, e, k0 in item_blocks(it):
                        if it["sample"]:
                            out, src = work[r, d, at * 256:at * 256 + WINDOW + SAMPLE], s_flat[r, at * 256:at * 256 + WINDOW + SAMPLE]
                            b = bias[r, 2 * hp + e, 2 * WINDOW - WINDOW - SAMPLE:2 * WINDOW]
                        else:
                            out, src = work[:, d, at * 256 + k0:at * 256 + 256], s_flat[:, at * 256 + k0:at * 256 + 256]
                            b = bias[:, 2 * hp + e, k0:256]
                        last = V.tensor_tensor_reduce(out=out, in0=src, in1=b, scale=HEAD_DIM ** -0.5, scalar=LOWEST, op0=ALU.add,
                                                      op1=ALU.max, accum_out=row_max[r, d, at:at + 1])
                    link(last)
                    h0 = 4 * g + 2 * hp
                    nt = nb // 2
                    m2 = lambda x: x[r, d, 0:nb].rearrange("p (t e) -> p t e", e=2)
                    ns = neg_sink[r, h0:h0 + 2].unsqueeze(1).to_broadcast([r.stop - r.start, nt, 2])
                    link(V.scalar_tensor_tensor(out=m2(neg_max), in0=m2(row_max), scalar=-1.0, in1=ns, op0=ALU.mult, op1=ALU.min))
                    V.tensor_tensor(m2(sink_arg), m2(neg_max), ns, ALU.subtract).then_inc(max_ready, 1)
                    dve.wait_ge(sink_ready, a + 1)
                    link(V.tensor_tensor(denom[r, d, 0:nb], row_sum[r, d, 0:nb], sink_exp[r, d, 0:nb], ALU.add))
                    V.reciprocal(recip[r, d, 0:nb], denom[r, d, 0:nb]).then_inc(recip_ready, 1)
                elif kind == "SPL":
                    it = items[st[1]]
                    a = it["a"]
                    dve.wait_ge(pt_hi_ready, a + 1)
                    o, e = span_of(it)
                    V.tensor_tensor(pt_lo[:, o:e], t_flat[:, o:e], pt_hi[:, o:e].bitcast(F32), ALU.subtract).then_inc(pt_lo_ready, 1)
                elif kind == "OG":
                    it = items[st[1]]
                    a, p, g, hp = it["a"], it["p"], it["g"], it["hp"]
                    n = 64 if it["sample"] else 512
                    dve.wait_ge(half_ready, a + 1)
                    link(V.tensor_tensor(ps_o[0:64, 0:n], ps_o[0:64, 0:n], h_half[:, 0:n], ALU.add))
                    gn = max(u["nth_anygate"] for u in units if u["kind"] == "agate" and u["p"] == p and u["g"] == g and u["i"] == hp)
                    dve.wait_ge(gate_ready, gn)
                    if a:
                        dve.wait_ge(yo_hi, a)
                        dve.wait_ge(yo_lo, a)
                    dve.wait_ge(ssum_done, 2 * p + 1)
                    tok, q = (PART, SAMPLE) if it["sample"] else (it["tiles"][0] * P, P)
                    nt = len(it["tiles"])
                    for e in range(2):
                        half = slice(64 * e, 64 * e + 64)
                        src = ps_o[0:64, 0:n].rearrange("p (t e c) -> p t e c", t=nt, e=2)[:, :, e, :]
                        dst = og[half, 0:nt * q].rearrange("p (t c) -> p t c", t=nt)
                        gt = silu_g[half, hp, tok:tok + nt * q].rearrange("p (t c) -> p t c", t=nt)
                        last = V.scalar_tensor_tensor(out=dst, in0=src, scalar=0.5, in1=gt, op0=ALU.mult, op1=ALU.mult)
                    last.then_inc(og_ready, 1)
                    dve.wait_ge(og_ready, a + 1)
                    dve.wait_ge(yo_hi, a + 1)
                    yt = 2 * g + hp
                    V.tensor_tensor(y_lo[:, yt, tok:tok + nt * q], og[:, 0:nt * q], y_hi[:, yt, tok:tok + nt * q].bitcast(F32),
                                    ALU.subtract).then_inc(yo_lo, 1)
                elif kind == "FT":
                    _, p, t = st
                    if t % 2 == 1:
                        n = ft_at[(p, t)]
                        dve.wait_ge(out_turned, n + 1)
                        dve.wait_ge(rstd_ready, norms(p, 2))
                        if n >= 2:
                            dve.wait_ge(y_stored[n % 2], 16 * (n // 2))
                        V.tensor_scalar(work[:, n % 2, :], t_flat, rstd[:, t:t + 1], None, ALU.mult).then_inc(out_dve, 1)

        @block.scalar
        def _(act):
            A = nc.scalar.activation
            act.wait_ge(prm_turned, 1)
            A(prm[:, :], t_flat[:, 0:R_ALL], ACT.Copy).then_inc(prm_ready, 1)
            act.wait_ge(prm_ready, 1)
            A(c_t[:, :], prm[:, R_C:R_C + 16], ACT.Tanh, scale=0.5).then_inc(c_tanh, 1)

            for st in steps:
                kind = st[0]
                if kind == "W":
                    j = st[1]
                    act.wait_ge(raw_loaded[j % 2], loads[j])
                    if j >= RING:
                        tile_used(act, j - RING)
                    A(w_hi[:, j % RING, 0:width[j]], w_raw[:, j % 2, 0:width[j]], ACT.Copy).then_inc(w_hi_ready, 1)
                elif kind == "MR":
                    m = st[1]
                    act.wait_ge(ada_done, KT * (m + 1))
                    if m:
                        act.wait_ge(mod_turned, m)
                    else:
                        act.wait_ge(prm_turned, 2)
                    for half in range(2):
                        last = A(mod_rows[:, 512 * half:512 * (half + 1)], mod_bank[m][half][0:2, :], ACT.Copy)
                    last.then_inc(mod_rows_ready, 1)
                elif kind == "XT":
                    _, p, t = st
                    n = xt_at[(p, t)]
                    c0, r0 = tok_span(t)
                    act.wait_ge(x_turned, n + 1)
                    if t % 2 == 0:
                        if p:
                            act.wait_ge(out_turned, ft_at[(p - 1, TILES - 1)] + 1 + (p == 1))
                        src = s_flat.rearrange("p (k c) -> p k c", k=KT)
                        A(x_res[:, :, c0 + r0:c0 + P], src[:, :, 0:P - r0], ACT.Copy).then_inc(x_put_act, 1)
                    if n == 0:
                        act.wait_ge(dve_const, 1)
                    if p and t == 0:
                        act.wait_ge(var_ready, norms(p - 1, 0))
                    A(x_in[r0:P, n % 2, :], x_in[r0:P, n % 2, :], ACT.Square, accum_out=ss[r0:P, t:t + 1]).then_inc(x_squared, 1)
                elif kind == "HS":
                    _, p, k = st
                    if k == 0:
                        act.wait_ge(x_put_dve, xt_dve[(p, TILES - 1)])
                        act.wait_ge(x_put_act, xt_act[(p, TILES if p == 0 else TILES - 2)])
                        act.wait_ge(mod_ready, mod_at[(0, 1)])
                    for c, w, v in spans(0, cols(p)):
                        last = A(h_hi[:, k, c:c + w], x_res[:, k, c:c + w], ACT.Copy, scale=gain[:, 0, k, v:v + 1])
                    last.then_inc(h_hi_ready, 1)
                elif kind == "NB":
                    _, p, r = st
                    act.wait_ge(rstd_spread, 2 * p + r + 1)
                    act.wait_ge(scaled, max([u["nth_proj"] for u in units if "nth_proj" in u and
                                             (u["p"] < p or (u["p"] == p and r and u["kind"] in ("u", "gate")))], default=0)) if (p or r) else None
                    last = A(rstd_b[:, 0:PART], ps_t[:, 0, :], ACT.Copy)
                    if p == 0:
                        last = A(rstd_b[:, PART:COLS], ps_t[:, 1, 0:SAMPLE], ACT.Copy)
                    last.then_inc(rb_ready, 1)
                elif kind == "E1":
                    u = units[st[1]]
                    p, c0, w, k = u["p"], u["c0"], u["w"], u["kind"]
                    bank = bank_of(u)
                    if k in ("u", "gate", "kv", "q", "agate"):
                        act.wait_ge(scaled, u["nth_proj"])
                        if k == "kv":
                            n = GROUPS * p + u["g"]
                            if n and u["b"] == 0:
                                act.wait_ge(v_turned, n)
                                act.wait_ge(k_lo_half, n)
                                act.wait_ge(k_prev, n)
                        if k == "u" and u["b"] == 0:
                            if u["p"] and u["g"] == 0 and u["i"] == 0:
                                act.wait_ge(rstd_spread, 2 * p + 1)
                            n = 8 * p + 2 * u["g"] + u["i"] - 1
                            if n >= 1:
                                act.wait_ge(pooled_ready, n)
                        for c, ww, v in spans(c0, w):
                            src = bank[:, c - c0:c - c0 + ww]
                            if k == "u":
                                at = c + U_PROMPT if v == 0 else c - PART + U_SAMPLE
                                dst = u_rows[u["i"]][:, at:at + ww]
                            elif k == "kv":
                                dst = kv_t[:, WINDOW + c:WINDOW + c + ww]
                            else:
                                dst = src
                            last = A(dst, src, ACT.Identity, bias=wb[:, u["n"], v:v + 1])
                        last.then_inc(biased, 1)
                        if k in ("gate", "agate"):
                            act.wait_ge(biased, u["nth_proj"])
                            if k == "gate":
                                n = 8 * p + 2 * u["g"] + u["i"]
                                before = [x for x in units if x["kind"] == "z" and 8 * x["p"] + x["n"] < n - 1 + 0 and x["u"] < u["u"]]
                                if before:
                                    act.wait_ge(y_ready, before[-1]["nth_z"])
                                if p and u["g"] == 0:
                                    act.wait_ge(og_ready, sum(1 for x in items if x["p"] < p))
                            else:
                                act.wait_ge(y_ready, sum(1 for x in units if x["kind"] == "z" and x["p"] <= p))
                                before = [x["a"] for x in items if x["hp"] == u["i"] and (x["p"], x["g"]) < (p, u["g"])]
                                if before:
                                    act.wait_ge(og_ready, before[-1] + 1)
                            A(silu_g[:, u["i"], c0:c0 + w], bank[:, 0:w], ACT.Tanh, scale=0.5).then_inc(tanh_ready, 1)
                        elif k == "q":
                            act.wait_ge(biased, u["nth_proj"])
                            before = [x["a"] for x in items if x["hp"] == u["i"] and (x["p"], x["g"]) < (p, u["g"])]
                            if before:
                                act.wait_ge(s_ready, before[-1] + 1)
                            for e in range(2):
                                last = A(q_st[0:64, 2 * u["i"] + e, c0:c0 + w], bank[64 * e:64 * e + 64, 0:w], ACT.Copy)
                            last.then_inc(q_hi_ready, 1)
                    elif k == "z":
                        act.wait_ge(y_ready, u["nth_z"])
                        A(y_hi[:, u["n"], c0:c0 + w], acc[:, c0:c0 + w], ACT.Copy).then_inc(yz_hi, 1)
                    else:
                        l, n = u["layer"], u["n"]
                        if u["b"] == len(sched.blocks(p)) - 1:
                            act.wait_ge(x_new, u["nth_out"])
                            i = 16 * p + 8 * l + n
                            if n:
                                act.wait_ge(acc_ready, i)
                            elif l == 0:
                                act.wait_ge(yz_lo, sum(1 for x in units if x["kind"] == "z" and x["p"] <= p))
                            else:
                                act.wait_ge(yo_lo, sum(1 for x in items if x["p"] <= p))
                                act.wait_ge(og_ready, sum(1 for x in items if x["p"] <= p))
                            A(sq[:, 0:cols(p)], x_res[:, n, 0:cols(p)], ACT.Square).then_inc(sq_ready, 1)
                            if l == 0:
                                act.wait_ge(mod_ready, mod_at[(1, 1)])
                                for c, ww, v in spans(0, cols(p)):
                                    last = A(h_hi[:, n, c:c + ww], x_res[:, n, c:c + ww], ACT.Copy, scale=gain[:, 1, n, v:v + 1])
                                last.then_inc(h_hi_ready, 1)
                            else:
                                act.wait_ge(sq_ready, i + 1)
                                A(x_res[:, n, 0:cols(p)], x_res[:, n, 0:cols(p)], ACT.Copy,
                                  scale=prm[:, R_FINAL + n:R_FINAL + n + 1]).then_inc(x_scaled, 1)
                elif kind == "PL":
                    _, p, g, i = st
                    n = 8 * p + 2 * g + i
                    act.wait_ge(pooled_ready, n + 1)
                    A(q_st[:, i, 0:cols(p)], sq[:, 0:cols(p)], ACT.Copy).then_inc(pooled_hi, 1)
                elif kind == "PS":
                    p = st[1]
                    act.wait_ge(state_turned, 1 if p == 0 else 2)
                    nat_free(act, ("state", p))
                    A(nat[:, :], ps_o[:, 0:P], ACT.Copy).then_inc(state_nat, 1)
                elif kind == "KS":
                    _, p, g = st
                    d, n = g % 2, GROUPS * p + g + 1
                    act.wait_ge(k_prev, n)
                    before = [x["a"] for x in items if GROUPS * x["p"] + x["g"] <= n - 3]
                    if before:
                        act.wait_ge(s_ready, before[-1] + 1)
                    a = 0 if p else WINDOW
                    last = A(k_hi[0:64, d, a:K_CACHE], kv_t[0:64, a:K_CACHE], ACT.Copy)
                    if p == 0:
                        last = A(k_hi[0:64, d, K_NEW:K_COLS], kv_t[0:64, K_CACHE:K_CACHE + SAMPLE], ACT.Copy)
                    last.then_inc(k_hi_half, 1)
                elif kind == "VT":
                    _, p, g = st
                    d, n = g % 2, GROUPS * p + g + 1
                    act.wait_ge(v_turned, n)
                    before = [x["a"] for x in items if GROUPS * x["p"] + x["g"] <= n - 3]
                    if before:
                        act.wait_ge(pv_done, before[-1] + 1)
                    src = t_flat.rearrange("p (b c) -> p b c", c=P)
                    a = 0 if p else 1
                    m = TILES + 1 - a
                    last = A(v_st[:, d, a:TILES + 1, 0:64], src[:, 0:m, 64:128], ACT.Copy)
                    if p == 0:
                        r = slice(P - SAMPLE, P)
                        A(v_st[r, d, TILES + 2, 0:64], src[r, 5, 64:128], ACT.Copy)
                        A(v_st[:, d, TILES + 1, 0:64], kv_cache[:, g, 64:128], ACT.Copy)
                        last = A(k_hi[0:64, d, K_CACHE:K_NEW], src[0:64, 4, :], ACT.Copy)
                    last.then_inc(v_hi_ready, 1)
                    act.wait_ge(v_hi_ready, n)
                    act.wait_ge(k_hi_half, n)
                    a, e = (0, K_CACHE) if p else (WINDOW, K_COLS)
                    A(k_hi[64:128, d, a:e], k_hi[0:64, d, a:e].bitcast(F32), ACT.Copy).then_inc(k_hi_ready, 1)
                elif kind == "SM":
                    it = items[st[1]]
                    a, d = it["a"], it["a"] % 2
                    r = slice(P - SAMPLE, P) if it["sample"] else slice(0, P)
                    nb = 2 * len(it["tiles"])
                    act.wait_ge(max_ready, a + 1)
                    if a >= 2:
                        act.wait_ge(recip_ready, a - 1)
                    for at, t, e, k0 in item_blocks(it):
                        x = work[r, d, at * 256 + k0:at * 256 + (WINDOW + SAMPLE if it["sample"] else 256)]
                        A(x, x, ACT.Exp, bias=neg_max[r, d, at:at + 1], accum_out=row_sum[r, d, at:at + 1])
                    A(sink_exp[r, d, 0:nb], sink_arg[r, d, 0:nb], ACT.Exp).then_inc(sink_ready, 1)
                elif kind == "SPL":
                    it = items[st[1]]
                    a = it["a"]
                    act.wait_ge(p_turned, a + 1)
                    if a:
                        act.wait_ge(pv_done, a)
                    o, e = span_of(it)
                    A(pt_hi[:, o:e], t_flat[:, o:e], ACT.Copy).then_inc(pt_hi_ready, 1)
                elif kind == "OG":
                    it = items[st[1]]
                    a, p = it["a"], it["p"]
                    n = 64 if it["sample"] else 512
                    act.wait_ge(pv_done, a + 1)
                    if a:
                        act.wait_ge(og_ready, a)
                    act.wait_ge(acc_ready, (2 * p + 1) * KT)
                    A(h_half[:, 0:n], ps_o[64:128, 0:n], ACT.Copy).then_inc(half_ready, 1)
                    act.wait_ge(og_ready, a + 1)
                    tok, q = (PART, SAMPLE) if it["sample"] else (it["tiles"][0] * P, P)
                    nt = len(it["tiles"])
                    A(y_hi[:, 2 * it["g"] + it["hp"], tok:tok + nt * q], og[:, 0:nt * q], ACT.Copy).then_inc(yo_hi, 1)
                elif kind == "FT":
                    _, p, t = st
                    if t % 2 == 0:
                        n = ft_at[(p, t)]
                        act.wait_ge(out_turned, n + 1)
                        act.wait_ge(rstd_ready, norms(p, 2))
                        if n >= 2:
                            act.wait_ge(y_stored[n % 2], 16 * (n // 2))
                        A(work[:, n % 2, :], s_flat, ACT.Copy, scale=rstd[:, t:t + 1]).then_inc(out_act, 1)

        @block.gpsimd
        def _(pool):
            G = nc.gpsimd
            G.memset(ident[:, :], 0.0).then_inc(pool_const, 1)
            pool.wait_ge(pool_const, 1)
            G.affine_select(out=ident[:, :], in_=ident[:, :], compare_op=ALU.not_equal, fill=1.0, base=0,
                            pattern=[[-1, P]], channel_multiplier=1).then_inc(pool_const, 1)
            G.iota(offsets.bitcast(I32), pattern=[[1, 2 * WINDOW]], base=-WINDOW, channel_multiplier=-1).then_inc(pool_const, 1)
            pool.wait_ge(dve_const, 2)
            split = 0
            for st in steps:
                kind = st[0]
                if kind == "W":
                    j = st[1]
                    split = j + 1
                    pool.wait_ge(w_hi_ready, j + 1)
                    pool.wait_ge(raw_loaded[j % 2], loads[j])
                    G.tensor_tensor(w_lo[:, j % RING, 0:width[j]], w_raw[:, j % 2, 0:width[j]],
                                    w_hi[:, j % RING, 0:width[j]].bitcast(F32), ALU.subtract).then_inc(w_lo_ready, 1)
                elif kind == "NA":
                    _, p, r = st
                    nt = TILES + (p == 0)
                    pool.wait_ge(var_ready, norms(p, r))
                    if p and r == 0:
                        f = ft_at[(p - 1, TILES - 1 + (p == 1))]
                        pool.wait_ge(out_act, sum(1 for x in ft[:f + 1] if x[2] % 2 == 0))
                        pool.wait_ge(out_dve, sum(1 for x in ft[:f + 1] if x[2] % 2 == 1))
                    if r:
                        pool.wait_ge(diag_ready, 2 * p + r)
                    G.tensor_tensor(rstd[:, 0:nt], var[:, 0:nt], power[:, 0:nt], ALU.pow).then_inc(rstd_ready, 1)
                elif kind == "E1" and units[st[1]]["kind"] == "out":
                    u = units[st[1]]
                    p, n = u["p"], u["n"]
                    if u["b"] == len(sched.blocks(p)) - 1:
                        i = 16 * p + 8 * u["layer"] + n
                        pool.wait_ge(sq_ready, i + 1)
                        w = cols(p)
                        if n:
                            pool.wait_ge(acc_ready, i)
                            G.tensor_tensor(acc[:, 0:w], acc[:, 0:w], sq[:, 0:w], ALU.add).then_inc(acc_ready, 1)
                        else:
                            if u["layer"] == 1 or p:
                                pool.wait_ge(ssum_done, 2 * p + u["layer"])
                            G.tensor_copy(acc[:, 0:w], sq[:, 0:w]).then_inc(acc_ready, 1)
                elif kind == "BI":
                    _, p, g, hp = st
                    before = [x["a"] for x in items if x["hp"] == hp and (x["p"], x["g"]) < (p, g)]
                    pool.wait_ge(mod_turned, len(sched.mods))
                    if before:
                        pool.wait_ge(max_ready, before[-1] + 1)
                    for e in range(2):
                        last = G.tensor_scalar(bias[:, 2 * hp + e, :], dist[:, :], -slope(4 * g + 2 * hp + e) * HEAD_DIM ** 0.5, 0.0,
                                               ALU.mult, ALU.add)
                    last.then_inc(bias_ready, 1)
                elif kind == "SM":
                    it = items[st[1]]
                    a, d = it["a"], it["a"] % 2
                    pool.wait_ge(recip_ready, a + 1)
                    pool.wait_ge(sink_ready, a + 1)
                    r = slice(P - SAMPLE, P) if it["sample"] else slice(0, P)
                    if it["sample"]:
                        pool.wait_ge(w_lo_ready, split)
                        pool.wait_ge(norm_ready, a)
                        pool.wait_ge(bias_ready, 8 * it["p"] + 2 * it["g"] + it["hp"] + 1)
                    for n, t in enumerate(it["tiles"]):
                        k0, w = (WINDOW, WINDOW) if (it["p"] == 0 and t == 0) else (0, 256)
                        if it["sample"]:
                            w = WINDOW + SAMPLE
                        x = work[r, d, n * 512:n * 512 + 512].rearrange("p (e c) -> p e c", e=2)[:, :, k0:k0 + w]
                        last = G.tensor_tensor(x, x, recip[r, d, 2 * n:2 * n + 2].unsqueeze(2).to_broadcast([r.stop - r.start, 2, w]), ALU.mult)
                    last.then_inc(norm_ready, 1)
                    if it["sample"]:
                        pool.wait_ge(norm_ready, a + 1)
                elif kind == "PS":
                    p = st[1]
                    out = O[5] if p == 0 else O[2]
                    pool.wait_ge(state_nat, 1 if p == 0 else 2)
                    for k in range(KT):
                        pool.dma_start(out[0, 0, :, k * P:(k + 1) * P], nat[k * HIST + 1:(k + 1) * HIST, :]).then_inc(nat_stored, 16)
                elif kind == "VT":
                    _, p, g = st
                    if p in (0, PARTS - 1):
                        pool.wait_ge(kv_nat, g + 1 + (4 if p else 0))
                        for i in range(2):
                            if p == 0:
                                pool.dma_start(O[6 + i][0, 0, WINDOW - SAMPLE:WINDOW, g, :], nat[P - SAMPLE:P, 64 * i:64 * i + 64]).then_inc(nat_stored, 16)
                            else:
                                pool.dma_start(O[3 + i][0, 0, :, g, :], nat[:, 64 * i:64 * i + 64]).then_inc(nat_stored, 16)
                elif kind == "FT":
                    _, p, t = st
                    n = ft_at[(p, t)]
                    if t % 2 == 0:
                        pool.wait_ge(out_act, ft_act[(p, t)])
                    else:
                        pool.wait_ge(out_dve, ft_dve[(p, t)])
                    if t == TILES:
                        pool.dma_start(O[1][0], work[P - SAMPLE:P, n % 2, :]).then_inc(y_stored[n % 2], 16)
                    else:
                        r0 = p * PART + t * P
                        pool.dma_start(O[0][0, r0:r0 + P, :], work[:, n % 2, :]).then_inc(y_stored[n % 2], 16)
            pool.wait_ge(nat_stored, sum(nat_size.values()))
            pool.wait_ge(y_stored[0], 16 * ((len(ft) + 1) // 2))
            pool.wait_ge(y_stored[1], 16 * (len(ft) // 2))


_INS = ['x_prompt', 'x_sample', 'c_prompt', 'c_sample', 'cache_pool', 'cache_k', 'cache_v', 'norm_g', 'ada_w', 'ada_b',
        'pool_w_in', 'pool_w_grp', 'pool_scale', 'pool_w_out', 'attn_w_in', 'attn_sinks', 'attn_w_out', 'final_g']
_KV = (1, 1, WINDOW, 4, HEAD_DIM)
_OUTS = [(1, SEQ, D_MODEL), (1, SAMPLE, D_MODEL), (1, 1, HIST - 1, D_MODEL), _KV, _KV, (1, 1, HIST - 1, D_MODEL), _KV, _KV]


def kernel(**inputs):
    import numpy as _np
    import concourse.bacc as _bacc
    from concourse.bass_utils import run_bass_kernel_spmd as _run

    nc = _bacc.Bacc("TRN2", target_bir_lowering=False, num_devices=1)
    arrays, ins = {}, {}
    for name in _INS:
        a = _np.ascontiguousarray(inputs[name])
        arrays[f"in_{name}_dram"] = a
        ins[name] = nc.dram_tensor(f"in_{name}_dram", a.shape, mybir.dt.from_np(a.dtype), kind="ExternalInput").ap()
    outs = [nc.dram_tensor(f"out_{i}_dram", shape, F32, kind="ExternalOutput").ap() for i, shape in enumerate(_OUTS)]
    trunk_kernel(nc, ins, outs)
    r = _run(nc, [arrays], core_ids=[0])
    return tuple(r.results[0][f"out_{i}_dram"] for i in range(len(_OUTS)))
```

```python
from contextlib import ExitStack

import concourse.bass as bass
from concourse import mybir

F32 = mybir.dt.float32
F32R = mybir.dt.float32r
I32 = mybir.dt.int32
ALU = mybir.AluOpType
ACT = mybir.ActivationFunctionType
AX_X = mybir.AxisListType.X

P = 128
D_MODEL = 1024
KT = D_MODEL // P
SEQ = 2048
PART = 512
PARTS = SEQ // PART
SAMPLE = 32
COLS = PART + SAMPLE
TILES = PART // P
GROUPS = 4
WINDOWS = (2, 4, 8, 16)
HIST = 16
HEADS = 16
HEAD_DIM = 64
WINDOW = 128
EPS = 1e-6
BIG = 1e33
RING = 4
AHEAD = 2
LANDING = 4
SHIFT = 2
LOWEST = -3e38

U_PROMPT = 2 * HIST
U_SAMPLE = U_PROMPT + PART + 2 * HIST
U_COLS = U_SAMPLE + SAMPLE
S_COLS = HIST + PART + HIST + SAMPLE
K_CACHE = WINDOW + PART
K_NEW = K_CACHE + WINDOW
K_COLS = K_NEW + SAMPLE
R_ADA_B, R_NORM, R_FINAL, R_POOL, R_C, R_ALL = 0, 48, 64, 72, 80, 96


def slope(h):
    return 2.0 ** (-8.0 * (h + 1) / HEADS)


def spans(c0, w):
    out = []
    if c0 < PART:
        out.append((c0, min(w, PART - c0), 0))
    if c0 + w > PART:
        s = max(c0, PART)
        out.append((s, c0 + w - s, 1))
    return out


class Schedule:

    def __init__(self):
        self.tiles, self.units, self.items, self.steps = [], [], [], []
        self.last_unit = {}
        self.mods = [(0, 1), (0, 0), (0, 2), (1, 1), (1, 0), (1, 2)]
        self.first = 2 * KT
        self.ada_next = 0
        self.splits = 0
        for p in range(PARTS):
            self.part(p)
        self.steps = [s for s in self.steps if s[0] != "W" or s[1] < len(self.tiles)]
        seen = {}
        for u in self.units:
            for kind in (u["kind"], "proj" if u["kind"] in ("u", "gate", "kv", "q", "agate") else None,
                         "anygate" if u["kind"] in ("gate", "agate") else None):
                if kind:
                    u["nth_" + kind] = seen.get(kind, 0) + 1
                    seen[kind] = seen.get(kind, 0) + 1

    def split_to(self, j):
        while self.splits <= j:
            self.steps.append(("W", self.splits))
            self.splits += 1

    def unit_group(self, p, tile, kind, ahead=True, **more):
        s = self.steps
        j = len(self.tiles)
        self.tiles.append(tile)
        if ahead:
            self.split_to(j + AHEAD)
        made = []
        for b, (c0, w) in enumerate(self.blocks(p)):
            made.append(self.unit(p, j, kind, b, c0, w, **more))
        self.last_unit[j] = made[-1]
        return made

    def ada(self, p):
        i = self.ada_next
        if p or i == KT * len(self.mods):
            return
        self.ada_next += 1
        self.steps.append(("ADA", i))
        if i % KT == KT - 1:
            self.steps.append(("MR", i // KT))
        elif i % KT == 1 and i // KT - 1 in (0, 2, 3):
            self.steps.append(("MT", i // KT - 1))

    def unit(self, p, j, kind, b, c0, w, **more):
        self.units.append(dict(u=len(self.units), p=p, j=j, kind=kind, b=b, c0=c0, w=w, **more))
        return len(self.units) - 1

    def blocks(self, p):
        return [(0, COLS // 2), (COLS // 2, COLS // 2)] if p == 0 else [(0, PART)]

    def part(self, p):
        s = self.steps
        n_tok = TILES + (p == 0)
        if p == 0:
            for t in range(2):
                s.append(("XL", p, t))
            for i in range(self.first):
                self.ada(p)
                if i == 1:
                    s.append(("HC",))
                if i % 2 == 0 and i // 2 - 1 in range(n_tok):
                    t = i // 2 - 1
                    s.append(("XT", p, t))
                    s.append(("XS", p, t))
                    if t + 2 < n_tok:
                        s.append(("XL", p, t + 2))
                if i >= self.first - 4:
                    for k in range(2):
                        s.append(("HS", p, 2 * (i - self.first + 4) + k))
            self.split_to(AHEAD - 1)
            s.append(("MT", 1))
            s.append(("SH", 0))
        else:
            for k in range(KT):
                s.append(("HS", p, k))
                if k in (1, 3):
                    s.append(("XS", p, 2 + k // 2))
        norm = [0]

        def emit(us, kind_evacs):
            for u in us:
                s.append(("U", u, 0, KT))
                norm[0] += 1
                if norm[0] <= 2:
                    s.append(("NA" if norm[0] == 1 else "NB", p, layer))
                    if norm[0] == 2:
                        for x in pending:
                            s.append(x)
                        pending.clear()
                e = [(k, u) for k in kind_evacs]
                if norm[0] < 2:
                    pending.extend(e)
                else:
                    s.extend(e)

        pending = []
        layer = 0
        if 0 < p < PARTS - 1:
            for t in range(2):
                s.append(("XL", p + 1, t))
        for g in range(GROUPS):
            for i in range(2):
                emit(self.unit_group(p, ("pin", 2 * g + i), "u", n=2 * g + i, g=g, i=i), ["E1"])
                if g or i:
                    self.ada(p)
                if i == 1:
                    s.append(("PL", p, g, 0))
            late = []
            for i in range(2):
                us = self.unit_group(p, ("pin", KT + 2 * g + i), "gate", n=KT + 2 * g + i, g=g, i=i)
                for u in us:
                    s.append(("U", u, 0, KT))
                    if i == 0:
                        if u == us[0]:
                            s.append(("PL", p, g, 1))
                    s.extend(late)
                    late = [("E2", u)]
                    s.append(("E1", u))
                self.ada(p)
            if g:
                self.ada(p)
            j = len(self.tiles)
            self.tiles.append(("grp", g))
            self.split_to(j + AHEAD)
            for m in range(2):
                for b, (c0, w) in enumerate(self.blocks(p)):
                    u = self.unit(p, j, "z", b, c0, w, n=2 * g + m, g=g, m=m)
                    s.append(("U", u, 0, KT))
                    s.extend(late)
                    late = [("E1", u)]
                    self.last_unit[j] = u
            s.extend(late)
        if p == 0:
            while self.ada_next < 5 * KT:
                self.ada(p)
            s.append(("MT", 4))
            s.append(("SH", 1))
        if p in (0, PARTS - 1):
            s.append(("PS", p))
        def out_units(name, layer, plan):
            late, order = [], []

            def finish(u, k0):
                s.append(("U", u, k0, KT))
                s.append(("E1", u))
                s.extend(late)
                late[:] = [("E2", u)] if layer == 0 else []

            for n in range(KT):
                j = len(self.tiles)
                us = self.unit_group(p, (name, n), "out", ahead=n > 0 and len(order) >= 3 or n == 0, n=n, layer=layer)
                fresh = us if len(order) >= 3 else us[3 - len(order):] if len(order) + len(us) > 3 else []
                before = len(order)
                order.extend(us)
                if before < 3 <= len(order):
                    done = [0, 0, 0]
                    for x in plan:
                        if isinstance(x, list):
                            s.extend(x)
                            continue
                        i, k0, k1 = x
                        s.append(("U", order[i], k0, k1))
                        done[i] = k1
                        if i == 0 and k0 == 0:
                            self.split_to(j + (1 if p else 2))
                    for i in range(3):
                        finish(order[i], done[i])
                        self.split_to(j + AHEAD)
                for u in fresh:
                    finish(u, 0)
                if layer == 0:
                    self.ada(p)
                if layer == 1 and p + 1 < PARTS and n in (4, 5):
                    s.append(("XS", p + 1, n - 4))
            s.extend(late)

        out_units("pout", 0, [(0, 0, 6), (1, 0, 6), (2, 0, 6)])
        if p == 0:
            s.append(("MT", 5))
            for t in range(2):
                s.append(("XL", p + 1, t))
        norm[0], layer = 0, 1
        kinds = [(0, 1), (2, 3)] + ([(4,)] if p == 0 else [])
        queue, to_norm = [None, None, None], []

        def item(g, hp, tiles):
            a = len(self.items)
            self.items.append(dict(a=a, p=p, g=g, hp=hp, tiles=tiles, sample=tiles == (4,)))
            return a

        def slot(a, evacs=(), before=(), after=()):
            first, second = [e for e in evacs if e[0] == "E1"], [e for e in evacs if e[0] == "E2"]
            out = list(before)
            if a is not None:
                early_bias = p > 0 and (self.items[a]["g"], self.items[a]["hp"]) == (0, 0)
                if self.items[a]["tiles"][0] == 0 and not early_bias:
                    out.append(("BI", p, self.items[a]["g"], self.items[a]["hp"]))
                out.append(("S", a))
            c, b = queue[0], queue[1]
            out += [("PV", c)] if c is not None else []
            out += first + to_norm + second
            out += [("OG", c)] if c is not None else []
            out += [("TR", b), ("PH", b)] if b is not None else []
            out += [("SM", a)] if a is not None else []
            out += [("split",)]
            out += [("YH", c)] if c is not None else []
            out += [("EX", a)] if a is not None else []
            out += [("PLO", b)] if b is not None else []
            out += [("YL", c)] if c is not None else []
            to_norm[:] = [("SR", a)] if a is not None else []
            out += list(after)
            queue.append(a)
            queue.pop(0)
            return out

        def rest(us, kinds_):
            for u in us:
                s.append(("U", u, 0, KT))
                norm[0] += 1
                if norm[0] in (1, 3):
                    s.append(("NA" if norm[0] == 1 else "NB", p, layer))
                evacs = [(k, u) for k in kinds_]
                if norm[0] < 3:
                    pending.extend(evacs)
                    evacs = []
                elif norm[0] == 3:
                    s.extend(pending)
                    pending.clear()
                if p == 0:
                    yield evacs
                elif u == us[-1]:
                    yield evacs

        if p == 0:
            places = {("q1", 1): 0, ("g0", 1): 1, ("g1", 0): 2, ("g1", 1): 3, ("kv", 1): 4, ("q0", 0): 5}
        else:
            places = {("q1", 0): 0, ("g0", 0): 1, ("g1", 0): 2, ("kv", 0): 3}
        old, new, early = [], [], []
        for g in range(GROUPS):
            n = 2 * KT + 5 * g
            for what, tile, kind, ks, more in (
                    ("kv", ("kv", g), "kv", ["E1"], dict(n=n, g=g)),
                    ("q0", ("ain", 256 * g), "q", ["E1", "E2"], dict(n=n + 1, g=g, i=0)),
                    ("q1", ("ain", 256 * g + P), "q", ["E1", "E2"], dict(n=n + 2, g=g, i=1)),
                    ("g0", ("ain", 1536 + 256 * g), "agate", ["E1", "E2"], dict(n=n + 3, g=g, i=0)),
                    ("g1", ("ain", 1536 + 256 * g + P), "agate", ["E1", "E2"], dict(n=n + 4, g=g, i=1))):
                if what == "q1":
                    old, new = new, [item(g, hp, t) for hp in range(2) for t in kinds]
                src = new
                j = len(self.tiles)
                us = self.unit_group(p, tile, kind, ahead=not (p and g == 0 and what == "q1"), **more)
                if p and g == 0 and kind != "agate":
                    early.append(us[0])
                    if what == "kv":
                        s.append(("BI", p, 0, 0))
                    s.append(("U", us[0], 0, KT - 1))
                    if what != "q1":
                        s.append(("NA" if what == "kv" else "NB", p, layer))
                        continue
                    kv, q0, q1 = early
                    norm[0] = 4
                    s.extend([("U", kv, KT - 1, KT), ("E1", kv), ("U", q0, KT - 1, KT), ("E1", q0), ("KS", p, g)])
                    s.extend([("U", q1, KT - 1, KT), ("VT", p, g), ("E2", q0)])
                    self.split_to(j + AHEAD)
                    continue
                elif p and g == 0 and kind == "agate":
                    if what == "g0":
                        s.append(("U", us[0], 0, KT - 2))
                        s.extend([x for x in slot(new[0]) if x != ("split",)])
                        s.append(("U", us[0], KT - 2, KT))
                        s.append(("E1", early[2]))
                        self.split_to(j + AHEAD + 1)
                        continue
                    else:
                        s.append(("U", us[0], 0, KT // 2))
                        s.extend([x for x in slot(new[1]) if x != ("split",)])
                        s.extend([("E2", early[2])] + [(e, us[0] - 1) for e in ks])
                        s.append(("U", us[0], KT // 2, KT))
                        blocks = [[(e, us[0]) for e in ks]]
                else:
                    blocks = rest(us, ks)
                for b, evacs in enumerate(blocks):
                    at = places.get((what, b))
                    a = src[at] if at is not None and src else None
                    last = b == (1 if p == 0 else 0)
                    before = [("KS", p, g)] if last and what == "q0" and g == 0 else []
                    if (what, b) == (("q0", 0) if p else ("q1", 0)):
                        before.append(("VT", p, g))
                    for x in slot(a, evacs, before, [("KS", p, g)] if last and what == "kv" and g else []):
                        if x == ("split",):
                            self.split_to(j + AHEAD + 1)
                        else:
                            s.append(x)
        tail = [new[at] for (what, b), at in places.items() if what in ("kv", "q0")]
        drain = [[x for x in slot(a) if x != ("split",)] for a in tail + [None, None, None]]
        begin = [(0, 0, 6), drain[0], (1, 0, 6), drain[1], (2, 0, 4), drain[2], (2, 4, 6)]
        if p == 0:
            begin.append(drain[3])
        out_units("aout", 1, begin + [(0, 6, 7), drain[-1], (1, 6, 7), (2, 6, 7)])
        s.append(("NA", p, 2))
        for t in (0, 1):
            s.append(("FT", p, t))
        for first in (0, 2):
            for t in range(first, first + 2 if first == 0 else n_tok):
                if first:
                    s.append(("FT", p, t))
                    s.append(("FO", p, t))
            if p + 1 < PARTS:
                for t in (first, first + 1):
                    s.append(("XT", p + 1, t))
                    if t < 2:
                        s.append(("XL", p + 1, t + 2))
            if not first:
                s.extend([("FO", p, 0), ("FO", p, 1)])


def trunk_kernel(nc, I, O):
    sched = Schedule()
    tiles, units, items, steps = sched.tiles, sched.units, sched.items, sched.steps

    with ExitStack() as ctx:
        def sb(name, shape, dt=F32):
            return ctx.enter_context(nc.sbuf_tensor(name, shape, dt))

        def ps(name, shape):
            return ctx.enter_context(nc.psum_tensor(name, shape, F32))

        def sem(name):
            return ctx.enter_context(nc.semaphore(name))

        x_res = sb("x_res", [P, KT, COLS])
        h_all_hi = sb("h_all_hi", [P, KT, SHIFT + COLS], F32R)
        h_all_lo = sb("h_all_lo", [P, KT, SHIFT + COLS], F32R)
        y_hi, y_lo = sb("y_hi", [P, KT, COLS], F32R), sb("y_lo", [P, KT, COLS], F32R)
        w_hi, w_lo = sb("w_hi", [P, RING, KT * P], F32R), sb("w_lo", [P, RING, KT * P], F32R)
        w_raw = sb("w_raw", [P, 2, KT * P])
        x_in = sb("x_in", [P, 2, D_MODEL])
        work = sb("work", [P, 2, 4 * 256])
        pt_hi, pt_lo = sb("pt_hi", [P, 1024], F32R), sb("pt_lo", [P, 1024], F32R)
        q_st = sb("q_st", [P, 4, COLS], F32R)
        kv_t = sb("kv_t", [P, WINDOW + COLS])
        k_hi, k_lo = sb("k_hi", [P, 2, K_COLS], F32R), sb("k_lo", [P, 2, K_COLS], F32R)
        v_st = sb("v_st", [P, 2, TILES + 3, P], F32R)
        silu_g = sb("silu_g", [P, 2, COLS])
        rstd_b = sb("rstd_b", [P, COLS])
        acc = sb("acc", [P, COLS])
        sq = sb("sq", [P, COLS])
        bias = sb("bias", [P, 4, 2 * WINDOW])
        dist = sb("dist", [P, 2 * WINDOW])
        kv_keep = sb("kv_keep", [P, GROUPS, WINDOW])
        kv_cache = sb("kv_cache", [P, GROUPS, P])
        u_keep, u_last = sb("u_keep", [P, KT, HIST]), sb("u_last", [P, KT, HIST])
        u_cache = sb("u_cache", [P, KT, HIST])
        nat = sb("nat", [P, P])
        ident, ones = sb("ident", [P, P]), sb("ones", [P, P])
        prm_rows, prm = sb("prm_rows", [P, P]), sb("prm", [P, R_ALL])
        c_t, c_s = sb("c_t", [P, 16]), sb("c_s", [P, 16])
        mod = sb("mod", [P, 2, 3 * KT, 2])
        gain = sb("gain", [P, 2, KT, 2])
        wb = sb("wb", [P, 2 * KT + 5 * GROUPS, 2])
        half_ps = sb("half_ps", [P, KT])
        inv_n = sb("inv_n", [P, GROUPS, HIST])
        ramp = sb("ramp", [P, HIST])
        head16 = sb("head16", [P, HIST])
        ss, var, rstd, power = sb("ss", [P, 5]), sb("var", [P, 5]), sb("rstd", [P, 5]), sb("power", [P, 5])
        sinks, neg_sink = sb("sinks", [P, HEADS]), sb("neg_sink", [P, HEADS])
        row_max, neg_max = sb("row_max", [P, 2, 4]), sb("neg_max", [P, 2, 4])
        row_sum, sink_arg, sink_exp = sb("row_sum", [P, 2, 4]), sb("sink_arg", [P, 2, 4]), sb("sink_exp", [P, 2, 4])
        denom, recip = sb("denom", [P, 2, 4]), sb("recip", [P, 2, 4])

        flat = work[:, :, :].rearrange("p a b -> p (a b)")
        u_rows = [flat[:, i * U_COLS:(i + 1) * U_COLS] for i in range(2)]
        win = flat[:, 2 * U_COLS:2 * U_COLS + S_COLS]
        diag = flat[:, 0:5 * P].rearrange("p (t c) -> p t c", t=5)
        h_hi, h_lo = h_all_hi[:, :, SHIFT:], h_all_lo[:, :, SHIFT:]
        og = acc[:, 0:256]
        bias_flat = bias[:, :, :].rearrange("p a b -> p (a b)")
        hist_rows, mod_rows = bias_flat[0:HIST - 1, :], bias_flat[0:2, :]
        out_rows = [work[:, 0, :], work[:, 1, :], silu_g[:, :, :].rearrange("p a b -> p (a b)")[:, 0:D_MODEL], bias_flat]
        offsets = kv_t[:, 0:2 * WINDOW]
        landing = [w_raw[:, 0, :], w_raw[:, 1, :], work[:, 0, :], work[:, 1, :], x_in[:, 0, :], x_in[:, 1, :]]
        c_pairs = c_s[:, :].rearrange("p (v k) -> p k v", v=2)
        h_half = sq[0:HEAD_DIM, 0:PART]

        ps_u = [ps(f"ps_u{i}", [P, 512]) for i in range(3)]
        ps_s, ps_t, ps_o = ps("ps_s", [P, 2, 512]), ps("ps_t", [P, 2, 512]), ps("ps_o", [P, 512])
        s_flat = ps_s[:, :, :].rearrange("p a b -> p (a b)")
        t_flat = ps_t[:, :, :].rearrange("p a b -> p (a b)")
        mod_bank = {0: (ps_u[0][:, :], ps_u[1][:, :]), 1: (ps_u[2][:, :], ps_o[:, :])}
        for m in range(2, 6):
            mod_bank[m] = (ps_s[:, 0, :], ps_s[:, 1, :])
        mod_turn = [ps_u[0] if m == 0 else ps_o for m in range(6)]

        const_loaded = sem("const_loaded")
        pool_const, dve_const = sem("pool_const"), sem("dve_const")
        prm_loaded = sem("prm_loaded")
        raw_loaded = [sem("raw_loaded0"), sem("raw_loaded1")]
        ada_loaded = [sem(f"ada_loaded{i}") for i in range(LANDING + 2)]
        mod_rows_ready, mod_turned, shift_ready = sem("mod_rows_ready"), sem("mod_turned"), sem("shift_ready")
        w_hi_ready, w_lo_ready, ada_done = sem("w_hi_ready"), sem("w_lo_ready"), sem("ada_done")
        prm_turned, prm_ready, c_tanh, c_ready, mod_ready = (
            sem("prm_turned"), sem("prm_ready"), sem("c_tanh"), sem("c_ready"), sem("mod_ready"))
        x_loaded = [sem("x_loaded0"), sem("x_loaded1")]
        x_turned, x_put_act, x_put_dve, x_squared = sem("x_turned"), sem("x_put_act"), sem("x_put_dve"), sem("x_squared")
        h_hi_ready, h_lo_ready = sem("h_hi_ready"), sem("h_lo_ready")
        ssum_done, var_ready, rstd_ready, diag_ready, rstd_spread, rb_ready = (
            sem("ssum_done"), sem("var_ready"), sem("rstd_ready"), sem("diag_ready"), sem("rstd_spread"), sem("rb_ready"))
        unit_done, scaled, biased, tanh_ready, gate_ready = (
            sem("unit_done"), sem("scaled"), sem("biased"), sem("tanh_ready"), sem("gate_ready"))
        pooled_ready, pooled_hi, pooled_lo = sem("pooled_ready"), sem("pooled_hi"), sem("pooled_lo")
        y_ready, yz_hi, yz_lo = sem("y_ready"), sem("yz_hi"), sem("yz_lo")
        x_new, sq_ready, acc_ready, x_scaled = sem("x_new"), sem("sq_ready"), sem("acc_ready"), sem("x_scaled")
        q_hi_ready, q_lo_ready = sem("q_hi_ready"), sem("q_lo_ready")
        k_prev, k_hi_half, k_lo_half, k_hi_ready, k_lo_ready = (
            sem("k_prev"), sem("k_hi_half"), sem("k_lo_half"), sem("k_hi_ready"), sem("k_lo_ready"))
        v_turned, v_hi_ready, v_lo_ready, kv_nat = (
            sem("v_turned"), sem("v_hi_ready"), sem("v_lo_ready"), sem("kv_nat"))
        bias_ready = sem("bias_ready")
        s_ready, max_ready, exp_ready, sink_ready, recip_ready, norm_ready = (
            sem("s_ready"), sem("max_ready"), sem("exp_ready"), sem("sink_ready"), sem("recip_ready"), sem("norm_ready"))
        p_turned, pt_hi_ready, pt_lo_ready, pv_done = (
            sem("p_turned"), sem("pt_hi_ready"), sem("pt_lo_ready"), sem("pv_done"))
        half_ready, og_ready, yo_hi, yo_lo = sem("half_ready"), sem("og_ready"), sem("yo_hi"), sem("yo_lo")
        state_turned, state_nat = sem("state_turned"), sem("state_nat")
        out_turned, out_act, out_dve = sem("out_turned"), sem("out_act"), sem("out_dve")
        nat_stored, cache_copied = sem("nat_stored"), sem("cache_copied")
        y_stored = [sem(f"y_stored{i}") for i in range(4)]
        dve_chain, act_chain = sem("dve_chain"), sem("act_chain")

        def tile_used(eng, j):
            eng.wait_ge(unit_done, sched.last_unit[j] + 1)

        first = sched.first
        mod_at = {m: i + 1 for i, m in enumerate(sched.mods)}

        def ada_slot(i):
            return (i % LANDING, i // LANDING + 1) if i < first else (LANDING + i % 2, (i - first) // 2 + 1)

        def bank_of(u):
            return ps_u[u["u"] % 3][:, shifts(u):512]

        def shifts(u):
            return SHIFT if u["p"] == 0 and u["b"] == 0 and u["kind"] in ("u", "gate", "kv", "q", "agate") else 0

        loads, per_slot = [], [0, 0]
        for j, t in enumerate(tiles):
            per_slot[j % 2] += 32 if t[0] == "kv" else 16
            loads.append(per_slot[j % 2])
        width = [2 * 2 * P if t[0] == "grp" else KT * P for t in tiles]
        def x_halves(p, t):
            if p and t > 1:
                return ("act", "dve")
            return ("act", "act") if t % 2 == 0 else ("dve", "dve")

        xt = [s for s in steps if s[0] == "XT"]
        xt_at = {s[1:]: n for n, s in enumerate(xt)}
        xt_act = {s[1:]: sum(1 for r in xt[:n + 1] if "act" in x_halves(*r[1:])) for n, s in enumerate(xt)}
        xt_dve = {s[1:]: sum(1 for r in xt[:n + 1] if "dve" in x_halves(*r[1:])) for n, s in enumerate(xt)}
        ft = [s for s in steps if s[0] == "FT"]
        ft_at = {s[1:]: n for n, s in enumerate(ft)}
        ft_act = {s[1:]: sum(1 for r in ft[:n + 1] if r[2] % 2 == 0) for n, s in enumerate(ft)}
        ft_dve = {s[1:]: sum(1 for r in ft[:n + 1] if r[2] % 2 == 1) for n, s in enumerate(ft)}
        out_unit = {(u["p"], u["layer"], u["n"], u["b"]): u for u in units if u["kind"] == "out"}
        nat_order = [("state", 0)] + [("kv", 0, g) for g in range(GROUPS)] \
            + [("state", PARTS - 1)] + [("kv", PARTS - 1, g) for g in range(GROUPS)]
        nat_size = {k: 8 * 16 if k[0] == "state" else 2 * 16 for k in nat_order}

        def nat_free(eng, key):
            before = sum(nat_size[k] for k in nat_order[:nat_order.index(key)])
            if before:
                eng.wait_ge(nat_stored, before)

        def rows_stored(eng, i, n):
            count = len([m for m in range(n) if m % 4 == i])
            if count:
                eng.wait_ge(y_stored[i], 16 * count)

        def norms(p, r):
            return 3 * p + r + 1

        def cols(p):
            return COLS if p == 0 else PART

        def tok_span(t):
            return (COLS - P, P - SAMPLE) if t == TILES else (t * P, 0)

        def x_banks(p, t):
            if p and t < 2:
                u = next(u["u"] for u in units if u["p"] == p)
                return ((ps_u[(u + 2) % 3], ps_u[(u + 1) % 3]) if t == 0 else (ps_o, ps_u[u % 3]))
            return (ps_t[:, 0, :], ps_t[:, 1, :]) if t % 2 else (ps_s[:, 0, :], ps_s[:, 1, :])

        def item_blocks(it):
            out = []
            for n, t in enumerate(it["tiles"]):
                for e in range(2):
                    out.append((2 * n + e, t, e, WINDOW if (it["p"] == 0 and t == 0) else 0))
            return out

        def span_of(it):
            if it["sample"]:
                return 0, 4 * SAMPLE
            return (256 if (it["p"] == 0 and it["tiles"][0] == 0) else 0), 1024

        z_until = {(p, k): sum(1 for x in units if x["kind"] == "z" and (x["p"], x["n"]) <= (p, k))
                   for p in range(PARTS) for k in range(KT)}
        item_until = {(p, k): sum(1 for x in items if (x["p"], 2 * x["g"] + x["hp"]) <= (p, k))
                      for p in range(PARTS) for k in range(KT)}

        block = ctx.enter_context(nc.Block())

        @block.sync
        def _(sp):
            def load_tile(j):
                t = tiles[j]
                dst = w_raw[:, j % 2, :].rearrange("p (k n) -> p k n", k=KT)
                if j >= 2:
                    sp.wait_ge(w_hi_ready, j - 1)
                    sp.wait_ge(w_lo_ready, j - 1)
                else:
                    sp.wait_ge(ada_done, first - LANDING + j + 1)
                s = raw_loaded[j % 2]
                if t[0] == "pin":
                    sp.dma_start(dst, I["pool_w_in"][0].rearrange("(k p) n -> p k n", p=P)[:, :, t[1] * P:(t[1] + 1) * P]).then_inc(s, 16)
                elif t[0] == "grp":
                    sp.dma_start(w_raw[:, j % 2, 0:4 * P].rearrange("p (k n) -> p k n", k=2),
                                 I["pool_w_grp"][0, t[1]].rearrange("(k p) n -> p k n", p=P)).then_inc(s, 16)
                elif t[0] == "pout":
                    sp.dma_start(dst, I["pool_w_out"][0].rearrange("(k p) n -> p k n", p=P)[:, :, t[1] * P:(t[1] + 1) * P]).then_inc(s, 16)
                elif t[0] == "aout":
                    sp.dma_start(dst, I["attn_w_out"][0].rearrange("(k p) n -> p k n", p=P)[:, :, t[1] * P:(t[1] + 1) * P]).then_inc(s, 16)
                elif t[0] == "ain":
                    sp.dma_start(dst, I["attn_w_in"][0].rearrange("(k p) n -> p k n", p=P)[:, :, t[1]:t[1] + P]).then_inc(s, 16)
                else:
                    src = I["attn_w_in"][0].rearrange("(k p) n -> p k n", p=P)
                    for half, at in enumerate((1024, 1280)):
                        sp.dma_start(dst[:, :, half * 64:half * 64 + 64],
                                     src[:, :, at + 64 * t[1]:at + 64 * t[1] + 64]).then_inc(s, 16)

            def load_ada(i):
                l, what = sched.mods[i // KT]
                half, pair = divmod(i % KT, 4)
                slot, nth = ada_slot(i)
                if i >= first:
                    sp.wait_ge(x_squared, TILES + 1)
                    if i >= first + 2:
                        sp.wait_ge(ada_done, i - 1)
                elif i >= LANDING:
                    sp.wait_ge(ada_done, i - LANDING + 1)
                at = what * D_MODEL + half * 512
                sp.dma_start(landing[slot].rearrange("p (k n) -> p k n", k=2),
                             I["ada_w"][l].rearrange("(k p) n -> p k n", p=P)[:, 2 * pair:2 * pair + 2, at:at + 512]).then_inc(ada_loaded[slot], 16)

            for name, at in (("ada_b", R_ADA_B), ("norm_g", R_NORM), ("final_g", R_FINAL), ("pool_scale", R_POOL),
                             ("c_prompt", R_C), ("c_sample", R_C + KT)):
                a = I[name] if name != "final_g" else I[name].rearrange("(o n) -> o n", o=1)
                rows = a.rearrange("l (k p) -> (l k) p", p=P)
                sp.dma_start(prm_rows[at:at + rows.shape[0], :], rows).then_inc(prm_loaded, 16)
            for i in range(LANDING):
                load_ada(i)
            sp.dma_start(hist_rows, I["cache_pool"][0, 0]).then_inc(const_loaded, 16)
            sp.dma_start(sinks[:, :], I["attn_sinks"].to_broadcast([P, HEADS])).then_inc(const_loaded, 16)
            sp.dma_start(kv_cache[:, :, 0:64], I["cache_k"][0, 0]).then_inc(const_loaded, 16)
            sp.dma_start(kv_cache[:, :, 64:128], I["cache_v"][0, 0]).then_inc(const_loaded, 16)
            sp.dma_start(O[6][0, 0, 0:WINDOW - SAMPLE], I["cache_k"][0, 0, SAMPLE:WINDOW]).then_inc(cache_copied, 16)
            sp.dma_start(O[7][0, 0, 0:WINDOW - SAMPLE], I["cache_v"][0, 0, SAMPLE:WINDOW]).then_inc(cache_copied, 16)
            for st in steps:
                if st[0] == "ADA":
                    i = st[1]
                    if i < first - LANDING:
                        load_ada(i + LANDING)
                    elif i < first - 2:
                        load_tile(i - first + LANDING)
                    elif i + 2 < KT * len(sched.mods):
                        load_ada(i + 2)
                elif st[0] == "W" and st[1] + 2 < len(tiles):
                    load_tile(st[1] + 2)
                elif st[0] == "XL":
                    _, p, t = st
                    n = xt_at[(p, t)]
                    if p == 1:
                        sp.wait_ge(ada_done, KT * len(sched.mods))
                    if n >= 2:
                        sp.wait_ge(x_squared, n - 1)
                        sp.wait_ge(x_turned, n - 1)
                    if t == TILES:
                        sp.dma_start(x_in[P - SAMPLE:P, n % 2, :], I["x_sample"][0]).then_inc(x_loaded[n % 2], 16)
                    else:
                        r0 = p * PART + t * P
                        sp.dma_start(x_in[:, n % 2, :], I["x_prompt"][0, r0:r0 + P, :]).then_inc(x_loaded[n % 2], 16)
                elif st[0] == "PS":
                    p = st[1]
                    out = O[5] if p == 0 else O[2]
                    sp.wait_ge(state_nat, 1 if p == 0 else 2)
                    for k in range(KT):
                        sp.dma_start(out[0, 0, :, k * P:(k + 1) * P], nat[k * HIST + 1:(k + 1) * HIST, :]).then_inc(nat_stored, 16)
                elif st[0] == "VT":
                    _, p, g = st
                    if p in (0, PARTS - 1):
                        sp.wait_ge(kv_nat, g + 1 + (4 if p else 0))
                        for i in range(2):
                            if p == 0:
                                sp.dma_start(O[6 + i][0, 0, WINDOW - SAMPLE:WINDOW, g, :], nat[P - SAMPLE:P, 64 * i:64 * i + 64]).then_inc(nat_stored, 16)
                            else:
                                sp.dma_start(O[3 + i][0, 0, :, g, :], nat[:, 64 * i:64 * i + 64]).then_inc(nat_stored, 16)
                elif st[0] == "FO":
                    _, p, t = st
                    n = ft_at[(p, t)]
                    if t % 2 == 0:
                        sp.wait_ge(out_act, ft_act[(p, t)])
                    else:
                        sp.wait_ge(out_dve, ft_dve[(p, t)])
                    if t == TILES:
                        sp.dma_start(O[1][0], out_rows[n % 4][P - SAMPLE:P, :]).then_inc(y_stored[n % 4], 16)
                    else:
                        r0 = p * PART + t * P
                        sp.dma_start(O[0][0, r0:r0 + P, :], out_rows[n % 4]).then_inc(y_stored[n % 4], 16)
            sp.wait_ge(cache_copied, 32)
            sp.wait_ge(nat_stored, sum(nat_size.values()))
            for i in range(4):
                rows_stored(sp, i, len(ft))


        @block.tensor
        def _(pe):
            free = {"s": [], "t": [], "o": []}

            def claim(bank, *readers):
                for s, v in free[bank]:
                    pe.wait_ge(s, v)
                free[bank] = list(readers)

            def split_product(out, pairs, first=True, final=True):
                n = 3 * len(pairs) + (not final)
                i = 0 if first else 1
                n += i
                for whi, wlo, xhi, xlo in pairs:
                    for w, x in ((whi, xhi), (whi, xlo), (wlo, xhi)):
                        last = nc.tensor.matmul(out, w, x, start=(i == 0), stop=(i == n - 1))
                        i += 1
                return last

            pe.wait_ge(prm_loaded, 6 * 16)
            pe.wait_ge(pool_const, 2)
            claim("t", (prm_ready, 1))
            nc.tensor.transpose(t_flat[:, 0:R_ALL], prm_rows[0:R_ALL, :], ident[0:R_ALL, 0:R_ALL]).then_inc(prm_turned, 1)
            pe.wait_ge(dve_const, 1)
            pe.wait_ge(c_ready, 1)

            for st in steps:
                kind = st[0]
                if kind == "HC":
                    pe.wait_ge(const_loaded, 4 * 16)
                    claim("s", (prm_ready, 2))
                    for k in range(KT):
                        last = nc.tensor.transpose(s_flat[:, k * HIST:k * HIST + HIST - 1], hist_rows[:, k * P:(k + 1) * P],
                                                   ident[0:HIST - 1, 0:HIST - 1])
                    last.then_inc(prm_turned, 1)
                elif kind == "ADA":
                    i = st[1]
                    m, half, pair = i // KT, i % KT // 4, i % 4
                    if m == 1 and i % KT == 0:
                        claim("o", (mod_ready, 2))
                    if m >= 2 and i % KT == 0:
                        claim("s", (mod_rows_ready, m + 1))
                    slot, nth = ada_slot(i)
                    pe.wait_ge(ada_loaded[slot], 16 * nth)
                    for k in range(2):
                        last = nc.tensor.matmul(mod_bank[m][half][0:2, :], c_pairs[:, 2 * pair + k, :],
                                                landing[slot][:, 512 * k:512 * (k + 1)],
                                                start=(pair == 0 and k == 0), stop=(pair == 3 and k == 1))
                    last.then_inc(ada_done, 1)
                elif kind == "MT":
                    m = st[1]
                    if m >= 2:
                        claim("o", (mod_ready, m + 1))
                    pe.wait_ge(mod_rows_ready, m + 1)
                    for k in range(KT):
                        last = nc.tensor.transpose(mod_turn[m][:, 2 * k:2 * k + 2], mod_rows[:, k * P:(k + 1) * P], ident[0:2, 0:2])
                    last.then_inc(mod_turned, 1)
                elif kind == "XT":
                    _, p, t = st
                    n = xt_at[(p, t)]
                    pe.wait_ge(x_loaded[n % 2], 16 * (n // 2 + 1))
                    _, r0 = tok_span(t)
                    if p and t == 1:
                        claim("o", (x_put_dve, xt_dve[(p, t)]))
                    elif p == 0 or t > 1:
                        readers = {"act": (x_put_act, xt_act[(p, t)]), "dve": (x_put_dve, xt_dve[(p, t)])}
                        claim("ts"[t % 2 == 0], *[readers[e] for e in sorted(set(x_halves(p, t)))])
                    if p and t < 2:
                        pe.wait_ge(x_new, next(u["nth_out"] for u in reversed(units) if u["kind"] == "out" and u["p"] == p - 1))
                    halves = x_banks(p, t)
                    for k in range(KT):
                        last = nc.tensor.transpose(halves[k // 4][:, k % 4 * P:(k % 4 + 1) * P - r0], x_in[r0:P, n % 2, k * P:(k + 1) * P],
                                                   ident[r0:P, r0:P])
                    last.then_inc(x_turned, 1)
                elif kind == "NA" and st[2] > 0:
                    _, p, r = st
                    claim("o", (var_ready, norms(p, r)))
                    pe.wait_ge(acc_ready, (2 * p + r) * (KT - 1))
                    pe.wait_ge(sq_ready, (2 * p + r) * KT)
                    for t in range(TILES + (p == 0)):
                        c0, _ = tok_span(t)
                        nc.tensor.matmul(ps_o[:, t:t + 1], acc[:, c0:c0 + P], ones[:, 0:1], start=True, stop=False)
                        last = nc.tensor.matmul(ps_o[:, t:t + 1], sq[:, c0:c0 + P], ones[:, 0:1], start=False, stop=True)
                    last.then_inc(ssum_done, 1)
                elif kind == "NB":
                    _, p, r = st
                    claim("t", (rb_ready, 2 * p + r + 1))
                    pe.wait_ge(diag_ready, 2 * p + r + 1)
                    last = nc.tensor.matmul(ps_t[:, 0, :], ones[:, :], flat[:, 0:PART], start=True, stop=True)
                    if p == 0:
                        last = nc.tensor.matmul(ps_t[:, 1, 0:SAMPLE], ones[:, :], diag[:, TILES, P - SAMPLE:P],
                                                start=True, stop=True)
                    last.then_inc(rstd_spread, 1)
                elif kind == "U":
                    u, k_from, k_to = units[st[1]], st[2], st[3]
                    p, j, c0, w = u["p"], u["j"], u["c0"], u["w"]
                    if u["u"] == 0:
                        pe.wait_ge(mod_ready, 1)
                    if u["u"] in (1, 2):
                        pe.wait_ge(mod_rows_ready, u["u"])
                    if p and u["kind"] in ("u", "gate") and u["g"] == 0:
                        pe.wait_ge(x_put_act, xt_act[(p, 0)])
                        pe.wait_ge(x_put_dve, xt_dve[(p, 1)])
                    if u["u"] >= 3:
                        v = units[u["u"] - 3]
                        if v["kind"] in ("u", "kv"):
                            pe.wait_ge(biased, v["nth_proj"])
                        elif v["kind"] in ("gate", "agate"):
                            pe.wait_ge(gate_ready, v["nth_anygate"])
                        elif v["kind"] == "q":
                            pe.wait_ge(q_lo_ready, v["nth_q"])
                        elif v["kind"] == "z":
                            pe.wait_ge(y_ready, v["nth_z"])
                        else:
                            pe.wait_ge(x_new, v["nth_out"])
                    pe.wait_ge(w_hi_ready, j + 1)
                    pe.wait_ge(w_lo_ready, j + 1)
                    bank = ps_u[u["u"] % 3]
                    slot = j % RING
                    if u["kind"] == "z":
                        pe.wait_ge(pooled_hi, 8 * p + 2 * u["g"] + 2)
                        pe.wait_ge(pooled_lo, 8 * p + 2 * u["g"] + 2)
                        at = [2 * P * k + P * u["m"] for k in range(2)]
                        last = split_product(bank[:, 0:w], [
                            (w_hi[:, slot, a:a + P], w_lo[:, slot, a:a + P], q_st[:, k, c0:c0 + w], q_st[:, 2 + k, c0:c0 + w])
                            for k, a in enumerate(at)])
                    else:
                        if u["kind"] == "out":
                            xh, xl = y_hi, y_lo
                        else:
                            xh, xl = h_all_hi, h_all_lo
                            c0, w = c0 + SHIFT - shifts(u), w + shifts(u)
                            if shifts(u):
                                pe.wait_ge(shift_ready, 1 if u["kind"] in ("u", "gate") else 2)
                        for k in range(k_from, k_to):
                            if u["kind"] != "out":
                                n = 16 * p + (0 if u["kind"] in ("u", "gate") else 8) + k + 1
                                pe.wait_ge(h_hi_ready, n)
                                pe.wait_ge(h_lo_ready, n)
                            elif u["layer"] == 0:
                                n = z_until[(p, k)]
                                pe.wait_ge(yz_hi, n)
                                pe.wait_ge(yz_lo, n)
                            else:
                                n = item_until[(p, k)]
                                pe.wait_ge(yo_hi, n)
                                pe.wait_ge(yo_lo, n)
                            last = split_product(bank[:, 0:w], [
                                (w_hi[:, slot, k * P:(k + 1) * P], w_lo[:, slot, k * P:(k + 1) * P],
                                 xh[:, k, c0:c0 + w], xl[:, k, c0:c0 + w])], k == 0, k == KT - 1)
                        if k_to < KT:
                            continue
                    last.then_inc(unit_done, 1)
                elif kind == "PS":
                    p = st[1]
                    claim("o", (state_nat, 1 if p == 0 else 2))
                    pe.wait_ge(pooled_ready, 8 * p + 8)
                    src = u_last if p == 0 else u_keep
                    nc.tensor.transpose(ps_o[:, 0:P], src[:, :, :].rearrange("p k c -> p (k c)"), ident[:, :]).then_inc(state_turned, 1)
                elif kind == "VT":
                    _, p, g = st
                    n = GROUPS * p + g + 1
                    claim("s", (v_lo_ready, n))
                    pe.wait_ge(biased, next(u["nth_proj"] for u in reversed(units)
                                            if u["kind"] == "kv" and u["p"] == p and u["g"] == g))
                    pe.wait_ge(k_prev, n)
                    first = 0 if p else 1
                    for b in range(TILES + 1 - first):
                        last = nc.tensor.transpose(s_flat[:, b * P:(b + 1) * P], kv_t[:, (first + b) * P:(first + b + 1) * P], ident[:, :])
                    if p == 0:
                        nc.tensor.transpose(s_flat[:, 4 * P:5 * P], kv_cache[:, g, :], ident[:, :])
                        last = nc.tensor.transpose(s_flat[:, 5 * P:6 * P], kv_t[:, COLS:COLS + P], ident[:, :])
                    last.then_inc(v_turned, 1)
                elif kind == "S":
                    it = items[st[1]]
                    a, p, g, d = it["a"], it["p"], it["g"], it["g"] % 2
                    claim("s", (max_ready, a + 1))
                    n = GROUPS * p + g + 1
                    pe.wait_ge(k_hi_ready, n)
                    pe.wait_ge(k_lo_ready, n)
                    qn = max(u["nth_q"] for u in units if u["kind"] == "q" and u["p"] == p and u["g"] == g and u["i"] == it["hp"])
                    pe.wait_ge(q_hi_ready, qn)
                    pe.wait_ge(q_lo_ready, qn)
                    for at, t, e, k0 in item_blocks(it):
                        c0, _ = tok_span(t)
                        if it["sample"]:
                            out, kc = s_flat[:, at * 256:at * 256 + WINDOW + SAMPLE], slice(K_CACHE, K_COLS)
                        else:
                            out, kc = s_flat[:, at * 256 + k0:at * 256 + 256], slice(t * P + k0, t * P + 256)
                        q = q_st[:, 2 * it["hp"] + e, c0:c0 + P]
                        nc.tensor.matmul(out, q, k_hi[:, d, kc], start=True, stop=False)
                        last = nc.tensor.matmul(out, q, k_lo[:, d, kc], start=False, stop=True)
                    last.then_inc(s_ready, 1)
                elif kind == "TR":
                    it = items[st[1]]
                    a = it["a"]
                    claim("t", (pt_lo_ready, a + 1))
                    pe.wait_ge(norm_ready, a + 1)
                    for at, t, e, k0 in item_blocks(it):
                        if it["sample"]:
                            r = slice(P - SAMPLE, P)
                            for kt in range(2):
                                o = (2 * kt + e) * SAMPLE
                                src = work[r, a % 2, at * 256 + kt * SAMPLE:at * 256 + kt * SAMPLE + P]
                                last = nc.tensor.transpose(t_flat[:, o:o + SAMPLE], src, ident[r, r])
                        else:
                            for kt in range(k0 // P, 2):
                                o = (4 * (at // 2) + 2 * kt + e) * P
                                last = nc.tensor.transpose(t_flat[:, o:o + P], work[:, a % 2, at * 256 + kt * P:at * 256 + (kt + 1) * P],
                                                           ident[:, :])
                    last.then_inc(p_turned, 1)
                elif kind == "PV":
                    it = items[st[1]]
                    a, p, g, d = it["a"], it["p"], it["g"], it["g"] % 2
                    claim("o", (og_ready, a + 1))
                    pe.wait_ge(pt_hi_ready, a + 1)
                    pe.wait_ge(pt_lo_ready, a + 1)
                    pe.wait_ge(v_hi_ready, GROUPS * p + g + 1)
                    pe.wait_ge(v_lo_ready, GROUPS * p + g + 1)
                    if it["sample"]:
                        r = slice(P - SAMPLE, P)
                        mms = [(v_st[:, d, TILES + 1, :], slice(0, P), 0), (v_st[r, d, TILES + 2, :], r, 64)]
                        i = 0
                        for v, rr, o in mms:
                            for pt in (pt_hi, pt_lo):
                                last = nc.tensor.matmul(ps_o[:, 0:64], v, pt[rr, o:o + 64], start=(i == 0), stop=(i == 3))
                                i += 1
                    else:
                        for n, t in enumerate(it["tiles"]):
                            kts = (1,) if (p == 0 and t == 0) else (0, 1)
                            i = 0
                            for kt in kts:
                                o = (4 * n + 2 * kt) * P
                                for pt in (pt_hi, pt_lo):
                                    last = nc.tensor.matmul(ps_o[:, n * 256:n * 256 + 256], v_st[:, d, t + kt, :], pt[:, o:o + 256],
                                                            start=(i == 0), stop=(i == 2 * len(kts) - 1))
                                    i += 1
                    last.then_inc(pv_done, 1)
                elif kind == "FT":
                    _, p, t = st
                    n = ft_at[(p, t)]
                    if t % 2 == 0:
                        claim("s", (out_act, ft_act[(p, t)]))
                    else:
                        claim("t", (out_dve, ft_dve[(p, t)]))
                    bank = (s_flat, t_flat)[t % 2]
                    pe.wait_ge(x_scaled, (p + 1) * KT)
                    c0, _ = tok_span(t)
                    for k in range(KT):
                        last = nc.tensor.transpose(bank[:, k * P:(k + 1) * P], x_res[:, k, c0:c0 + P], ident[:, :])
                    last.then_inc(out_turned, 1)

        @block.vector
        def _(dve):
            n_chain = [0]

            def link(ins):
                n_chain[0] += 1
                ins.then_inc(dve_chain, 1)
                dve.wait_ge(dve_chain, n_chain[0])

            V = nc.vector
            V.memset(ones[:, :], 1.0)
            V.memset(power[:, :], -0.5)
            V.memset(u_keep[:, :, :], 0.0)
            V.memset(u_cache[:, :, :], 0.0)
            V.memset(ss[:, :], 1.0).then_inc(dve_const, 1)
            for t in range(HIST):
                last = V.memset(ramp[:, t:t + 1], float(t + 1))
            link(last)
            for g in range(GROUPS):
                last = V.tensor_scalar(inv_n[:, g, :], ramp[:, :], float(WINDOWS[g]), None, ALU.min)
            link(last)
            link(V.reciprocal(inv_n[:, :, :], inv_n[:, :, :]))
            dve.wait_ge(pool_const, 3)
            link(V.tensor_copy(dist[:, :], offsets.bitcast(I32)))
            link(V.scalar_tensor_tensor(out=dist[:, :], in0=dist[:, :], scalar=-1.0, in1=dist[:, :], op0=ALU.mult, op1=ALU.max))
            V.memset(dist[0:64, 192:256], BIG)
            V.memset(dist[64:128, 0:64], BIG).then_inc(dve_const, 1)
            dve.wait_ge(c_tanh, 1)
            link(V.scalar_tensor_tensor(out=c_s[:, :], in0=c_t[:, :], scalar=1.0, in1=prm[:, R_C:R_C + 16], op0=ALU.add, op1=ALU.mult))
            V.tensor_scalar(c_s[:, :], c_s[:, :], 0.5, None, ALU.mult).then_inc(c_ready, 1)
            link(V.tensor_scalar(half_ps[:, :], prm[:, R_POOL:R_POOL + KT], 0.5, None, ALU.mult))

            for st in steps:
                kind = st[0]
                if kind == "HC":
                    dve.wait_ge(const_loaded, 4 * 16)
                    link(V.tensor_scalar(neg_sink[:, :], sinks[:, :], -1.0, None, ALU.mult))
                    dve.wait_ge(prm_turned, 2)
                    V.tensor_copy(u_cache[:, :, 1:HIST], s_flat[:, 0:KT * HIST].rearrange("p (k c) -> p k c", k=KT)[:, :, 0:HIST - 1]).then_inc(prm_ready, 1)
                elif kind == "MT":
                    m = st[1]
                    l, what = sched.mods[m]
                    ns = slice(KT * what, KT * (what + 1))
                    dve.wait_ge(mod_turned, m + 1)
                    add = V.tensor_tensor(mod[:, l, ns, :], mod_turn[m][:, 0:2 * KT].rearrange("p (n v) -> p n v", v=2),
                                          prm[:, R_ADA_B + 24 * l + KT * what:R_ADA_B + 24 * l + KT * (what + 1)]
                                          .unsqueeze(2).to_broadcast([P, KT, 2]), ALU.add)
                    if what == 1:
                        link(add)
                        add = V.scalar_tensor_tensor(out=gain[:, l], in0=mod[:, l, ns, :], scalar=1.0,
                                                     in1=prm[:, R_NORM + KT * l:R_NORM + KT * (l + 1)].unsqueeze(2).to_broadcast([P, KT, 2]),
                                                     op0=ALU.add, op1=ALU.mult)
                    add.then_inc(mod_ready, 1)
                    dve.wait_ge(mod_ready, m + 1)
                elif kind == "SH":
                    l = st[1]
                    if l:
                        dve.wait_ge(unit_done, 1 + next(u["u"] for u in reversed(units) if u["kind"] == "gate" and u["p"] == 0))
                    link(V.tensor_copy(h_all_hi[:, :, 0:SHIFT], mod[:, l, 0:KT, :]))
                    V.tensor_tensor(h_all_lo[:, :, 0:SHIFT], mod[:, l, 0:KT, :], h_all_hi[:, :, 0:SHIFT].bitcast(F32),
                                    ALU.subtract).then_inc(shift_ready, 1)
                elif kind == "XT":
                    _, p, t = st
                    if "dve" in x_halves(p, t):
                        dve.wait_ge(x_turned, xt_at[(p, t)] + 1)
                        if p:
                            dve.wait_ge(out_turned, ft_at[(p - 1, t + (p == 1 and t == TILES - 1))] + 1)
                        for half, bank in enumerate(x_banks(p, t)):
                            if x_halves(p, t)[half] == "dve":
                                last = V.tensor_copy(x_res[:, 4 * half:4 * half + 4, t * P:(t + 1) * P], bank[:, :].rearrange("p (k c) -> p k c", k=4))
                        last.then_inc(x_put_dve, 1)
                elif kind == "HS":
                    _, p, k = st
                    dve.wait_ge(h_hi_ready, 16 * p + k + 1)
                    if k == 0:
                        dve.wait_ge(x_put_dve, xt_dve[(p, TILES - 1)])
                        dve.wait_ge(x_put_act, xt_act[(p, TILES if p == 0 else TILES - 1)])
                    for c, w, v in spans(0, cols(p)):
                        last = V.scalar_tensor_tensor(out=h_lo[:, k, c:c + w], in0=x_res[:, k, c:c + w], scalar=gain[:, 0, k, v:v + 1],
                                                      in1=h_hi[:, k, c:c + w].bitcast(F32), op0=ALU.mult, op1=ALU.subtract)
                    last.then_inc(h_lo_ready, 1)
                elif kind == "NA":
                    _, p, r = st
                    nt = TILES + (p == 0)
                    if r == 0:
                        dve.wait_ge(x_squared, xt_at[(p, nt - 1)] + 1)
                        src = ss[:, 0:nt]
                    else:
                        dve.wait_ge(ssum_done, 2 * p + r)
                        src = ps_o[:, 0:nt]
                    if 3 * p + r:
                        dve.wait_ge(rstd_ready, norms(p, r) - 1)
                    V.tensor_scalar(var[:, 0:nt], src, 1.0 / D_MODEL, EPS, ALU.mult, ALU.add).then_inc(var_ready, 1)
                    if r < 2:
                        dve.wait_ge(rstd_ready, norms(p, r))
                        if r:
                            dve.wait_ge(unit_done, next(u["u"] for u in reversed(units) if u["kind"] == "z" and u["p"] == p))
                        elif p:
                            n_items = sum(1 for x in items if x["p"] < p)
                            dve.wait_ge(p_turned, n_items)
                            for i in range(2):
                                rows_stored(dve, i, ft_at[(p - 1, TILES - 1 + (p == 1))] + 1)
                        V.tensor_tensor(diag[:, 0:nt, :], ident[:, :].unsqueeze(1).to_broadcast([P, nt, P]),
                                        rstd[:, 0:nt].unsqueeze(2).to_broadcast([P, nt, P]), ALU.mult).then_inc(diag_ready, 1)
                elif kind == "E1":
                    u = units[st[1]]
                    p, c0, w, k = u["p"], u["c0"], u["w"], u["kind"]
                    bank = bank_of(u)
                    dve.wait_ge(unit_done, u["u"] + 1)
                    if k in ("u", "gate", "kv", "q", "agate"):
                        if p == 0 and u["b"] == 0:
                            V.tensor_copy(wb[:, u["n"], :], ps_u[u["u"] % 3][:, 0:SHIFT])
                        dve.wait_ge(rb_ready, 2 * p + (1 if k in ("u", "gate") else 2))
                        V.tensor_tensor(bank[:, 0:w], bank[:, 0:w], rstd_b[:, c0:c0 + w], ALU.mult).then_inc(scaled, 1)
                    elif k == "z":
                        i = u["m"]
                        gates = [x for x in units if x["kind"] == "gate" and x["p"] == p and x["g"] == u["g"] and x["i"] == i and x["b"] == u["b"]]
                        dve.wait_ge(gate_ready, gates[0]["nth_anygate"])
                        if u["nth_z"] > 1:
                            dve.wait_ge(yz_hi, u["nth_z"] - 1)
                            dve.wait_ge(yz_lo, u["nth_z"] - 1)
                        if p:
                            dve.wait_ge(yo_hi, sum(1 for x in items if x["p"] < p))
                            dve.wait_ge(yo_lo, sum(1 for x in items if x["p"] < p))
                        V.scalar_tensor_tensor(out=acc[:, c0:c0 + w], in0=bank[:, 0:w], scalar=half_ps[:, u["n"]:u["n"] + 1],
                                               in1=silu_g[:, i, c0:c0 + w], op0=ALU.mult, op1=ALU.mult).then_inc(y_ready, 1)
                        dve.wait_ge(yz_hi, u["nth_z"])
                        dve.wait_ge(y_ready, u["nth_z"])
                        V.tensor_tensor(y_lo[:, u["n"], c0:c0 + w], acc[:, c0:c0 + w], y_hi[:, u["n"], c0:c0 + w].bitcast(F32),
                                        ALU.subtract).then_inc(yz_lo, 1)
                    else:
                        l, n = u["layer"], u["n"]
                        for c, ww, v in spans(c0, w):
                            last = V.scalar_tensor_tensor(out=x_res[:, n, c:c + ww], in0=bank[:, c - c0:c - c0 + ww],
                                                          scalar=mod[:, l, 2 * KT + n, v:v + 1], in1=x_res[:, n, c:c + ww],
                                                          op0=ALU.mult, op1=ALU.add)
                        last.then_inc(x_new, 1)
                elif kind == "E2":
                    u = units[st[1]]
                    p, c0, w, k = u["p"], u["c0"], u["w"], u["kind"]
                    bank = bank_of(u)
                    if k in ("gate", "agate"):
                        dve.wait_ge(tanh_ready, u["nth_anygate"])
                        V.scalar_tensor_tensor(out=silu_g[:, u["i"], c0:c0 + w], in0=silu_g[:, u["i"], c0:c0 + w], scalar=1.0,
                                               in1=bank[:, 0:w], op0=ALU.add, op1=ALU.mult).then_inc(gate_ready, 1)
                    elif k == "q":
                        dve.wait_ge(q_hi_ready, u["nth_q"])
                        for e in range(2):
                            q = q_st[:, 2 * u["i"] + e, c0:c0 + w]
                            last = V.tensor_tensor(q[64:128], bank[64 * e:64 * e + 64, 0:w], q[0:64].bitcast(F32), ALU.subtract)
                        last.then_inc(q_lo_ready, 1)
                    else:
                        n = u["n"]
                        if u["b"] == len(sched.blocks(p)) - 1:
                            dve.wait_ge(h_hi_ready, 16 * p + 8 + n + 1)
                            for c, ww, v in spans(0, cols(p)):
                                last = V.scalar_tensor_tensor(out=h_lo[:, n, c:c + ww], in0=x_res[:, n, c:c + ww],
                                                              scalar=gain[:, 1, n, v:v + 1], in1=h_hi[:, n, c:c + ww].bitcast(F32),
                                                              op0=ALU.mult, op1=ALU.subtract)
                            last.then_inc(h_lo_ready, 1)
                elif kind == "PL":
                    _, p, g, i = st
                    n = 8 * p + 2 * g + i
                    row, wdw = u_rows[i], WINDOWS[g]
                    dve.wait_ge(biased, next(x["nth_proj"] for x in reversed(units)
                                             if x["kind"] == "u" and x["p"] == p and x["g"] == g and x["i"] == i))
                    V.memset(row[:, 0:HIST], 0.0)
                    link(V.tensor_copy(row[:, HIST:2 * HIST], u_keep[:, 2 * g + i, :]))
                    if p == 0:
                        V.memset(row[:, U_PROMPT + PART:U_PROMPT + PART + HIST], 0.0)
                        link(V.tensor_copy(row[:, U_SAMPLE - HIST:U_SAMPLE], u_cache[:, 2 * g + i, :]))
                        V.tensor_copy(u_last[:, 2 * g + i, :], row[:, U_COLS - HIST:U_COLS])
                    V.tensor_copy(u_keep[:, 2 * g + i, :], row[:, U_PROMPT + PART - HIST:U_PROMPT + PART])
                    last = V.tensor_tensor_scan(win[:, 0:HIST + PART], row[:, HIST:U_PROMPT + PART],
                                                row[:, HIST - wdw:U_PROMPT + PART - wdw], 0.0, ALU.add, ALU.subtract)
                    if p == 0:
                        last = V.tensor_tensor_scan(win[:, HIST + PART:S_COLS], row[:, U_SAMPLE - HIST:U_COLS],
                                                    row[:, U_SAMPLE - HIST - wdw:U_COLS - wdw], 0.0, ALU.add, ALU.subtract)
                    link(last)
                    if n:
                        dve.wait_ge(pooled_hi, n)
                        dve.wait_ge(pooled_lo, n)
                    if p:
                        dve.wait_ge(ssum_done, 2 * p)
                    first = 0
                    if p == 0:
                        first = HIST
                        link(V.tensor_tensor(head16[:, :], win[:, HIST:2 * HIST], inv_n[:, g, :], ALU.mult))
                        V.tensor_tensor(sq[:, 0:HIST], head16[:, :], row[:, U_PROMPT:U_PROMPT + HIST], ALU.subtract)
                        V.scalar_tensor_tensor(out=sq[:, PART:COLS], in0=win[:, 2 * HIST + PART:S_COLS], scalar=1.0 / wdw,
                                               in1=row[:, U_SAMPLE:U_COLS], op0=ALU.mult, op1=ALU.subtract)
                    V.scalar_tensor_tensor(out=sq[:, first:PART], in0=win[:, HIST + first:HIST + PART], scalar=1.0 / wdw,
                                           in1=row[:, U_PROMPT + first:U_PROMPT + PART], op0=ALU.mult, op1=ALU.subtract).then_inc(pooled_ready, 1)
                    dve.wait_ge(pooled_ready, n + 1)
                    dve.wait_ge(pooled_hi, n + 1)
                    V.tensor_tensor(q_st[:, 2 + i, 0:cols(p)], sq[:, 0:cols(p)], q_st[:, i, 0:cols(p)].bitcast(F32),
                                    ALU.subtract).then_inc(pooled_lo, 1)
                elif kind == "KS":
                    _, p, g = st
                    d, n = g % 2, GROUPS * p + g + 1
                    dve.wait_ge(biased, next(u["nth_proj"] for u in reversed(units)
                                             if u["kind"] == "kv" and u["p"] == p and u["g"] == g))
                    if n > 1:
                        dve.wait_ge(v_turned, n - 1)
                        dve.wait_ge(k_hi_half, n - 1)
                        dve.wait_ge(k_lo_half, n - 1)
                    if p:
                        link(V.tensor_copy(kv_t[:, 0:WINDOW], kv_keep[:, g, :]))
                    V.tensor_copy(kv_keep[:, g, :], kv_t[:, PART:PART + WINDOW]).then_inc(k_prev, 1)
                    dve.wait_ge(k_prev, n)
                    dve.wait_ge(k_hi_half, n)
                    a = 0 if p else WINDOW
                    last = V.tensor_tensor(k_lo[0:64, d, a:K_CACHE], kv_t[0:64, a:K_CACHE], k_hi[0:64, d, a:K_CACHE].bitcast(F32), ALU.subtract)
                    if p == 0:
                        last = V.tensor_tensor(k_lo[0:64, d, K_NEW:K_COLS], kv_t[0:64, K_CACHE:K_CACHE + SAMPLE],
                                               k_hi[0:64, d, K_NEW:K_COLS].bitcast(F32), ALU.subtract)
                    last.then_inc(k_lo_half, 1)
                elif kind == "VT":
                    _, p, g = st
                    d, n = g % 2, GROUPS * p + g + 1
                    dve.wait_ge(v_hi_ready, n)
                    dve.wait_ge(v_turned, n)
                    src = s_flat.rearrange("p (b c) -> p b c", c=P)
                    a = 0 if p else 1
                    m = TILES + 1 - a
                    r = slice(P - SAMPLE, P)
                    if p == 0:
                        V.tensor_tensor(v_st[r, d, TILES + 2, 64:128], src[r, 5, 64:128], v_st[r, d, TILES + 2, 0:64].bitcast(F32), ALU.subtract)
                        V.tensor_tensor(v_st[:, d, TILES + 1, 64:128], kv_cache[:, g, 64:128], v_st[:, d, TILES + 1, 0:64].bitcast(F32), ALU.subtract)
                        V.tensor_tensor(k_lo[0:64, d, K_CACHE:K_NEW], src[0:64, 4, :], k_hi[0:64, d, K_CACHE:K_NEW].bitcast(F32), ALU.subtract)
                    if p in (0, PARTS - 1):
                        nat_free(dve, ("kv", p, g))
                        if g == 0:
                            dve.wait_ge(state_nat, 1 if p == 0 else 2)
                        rows, b = (r, 5) if p == 0 else (slice(0, P), TILES)
                        V.tensor_copy(nat[rows, :], src[rows, b, :]).then_inc(kv_nat, 1)
                        dve.wait_ge(kv_nat, g + 1 + (4 if p else 0))
                    V.tensor_tensor(v_st[:, d, a:TILES + 1, 64:128], src[:, 0:m, 64:128],
                                    v_st[:, d, a:TILES + 1, 0:64].bitcast(F32), ALU.subtract).then_inc(v_lo_ready, 1)
                    dve.wait_ge(v_lo_ready, n)
                    a, e = (0, K_CACHE) if p else (WINDOW, K_COLS)
                    V.tensor_copy(k_lo[64:128, d, a:e], k_lo[0:64, d, a:e].bitcast(F32)).then_inc(k_lo_ready, 1)
                elif kind == "SM":
                    it = items[st[1]]
                    a, g, hp = it["a"], it["g"], it["hp"]
                    d = a % 2
                    nb = 2 * len(it["tiles"])
                    r = slice(P - SAMPLE, P) if it["sample"] else slice(0, P)
                    dve.wait_ge(s_ready, a + 1)
                    dve.wait_ge(bias_ready, 8 * it["p"] + 2 * g + hp + 1)
                    if a >= 2:
                        dve.wait_ge(p_turned, a - 1)
                    for at, t, e, k0 in item_blocks(it):
                        if it["sample"]:
                            out, src = work[r, d, at * 256:at * 256 + WINDOW + SAMPLE], s_flat[r, at * 256:at * 256 + WINDOW + SAMPLE]
                            b = bias[r, 2 * hp + e, 2 * WINDOW - WINDOW - SAMPLE:2 * WINDOW]
                        else:
                            out, src = work[:, d, at * 256 + k0:at * 256 + 256], s_flat[:, at * 256 + k0:at * 256 + 256]
                            b = bias[:, 2 * hp + e, k0:256]
                        last = V.tensor_tensor_reduce(out=out, in0=src, in1=b, scale=HEAD_DIM ** -0.5, scalar=LOWEST, op0=ALU.add,
                                                      op1=ALU.max, accum_out=row_max[r, d, at:at + 1])
                    link(last)
                    h0 = 4 * g + 2 * hp
                    nt = nb // 2
                    m2 = lambda x: x[r, d, 0:nb].rearrange("p (t e) -> p t e", e=2)
                    ns = neg_sink[r, h0:h0 + 2].unsqueeze(1).to_broadcast([r.stop - r.start, nt, 2])
                    link(V.scalar_tensor_tensor(out=m2(neg_max), in0=m2(row_max), scalar=-1.0, in1=ns, op0=ALU.mult, op1=ALU.min))
                    V.tensor_tensor(m2(sink_arg), m2(neg_max), ns, ALU.subtract).then_inc(max_ready, 1)
                elif kind == "SR":
                    it = items[st[1]]
                    a, d = it["a"], it["a"] % 2
                    nb = 2 * len(it["tiles"])
                    r = slice(P - SAMPLE, P) if it["sample"] else slice(0, P)
                    dve.wait_ge(sink_ready, a + 1)
                    link(V.tensor_tensor(denom[r, d, 0:nb], row_sum[r, d, 0:nb], sink_exp[r, d, 0:nb], ALU.add))
                    V.reciprocal(recip[r, d, 0:nb], denom[r, d, 0:nb]).then_inc(recip_ready, 1)
                elif kind == "PLO":
                    it = items[st[1]]
                    a = it["a"]
                    dve.wait_ge(pt_hi_ready, a + 1)
                    o, e = span_of(it)
                    V.tensor_tensor(pt_lo[:, o:e], t_flat[:, o:e], pt_hi[:, o:e].bitcast(F32), ALU.subtract).then_inc(pt_lo_ready, 1)
                elif kind == "OG":
                    it = items[st[1]]
                    a, p, g, hp = it["a"], it["p"], it["g"], it["hp"]
                    n = 64 if it["sample"] else 512
                    dve.wait_ge(half_ready, a + 1)
                    link(V.tensor_tensor(ps_o[0:64, 0:n], ps_o[0:64, 0:n], h_half[:, 0:n], ALU.add))
                    gn = max(u["nth_anygate"] for u in units if u["kind"] == "agate" and u["p"] == p and u["g"] == g and u["i"] == hp)
                    dve.wait_ge(gate_ready, gn)
                    if a:
                        dve.wait_ge(yo_hi, a)
                        dve.wait_ge(yo_lo, a)
                    dve.wait_ge(ssum_done, 2 * p + 1)
                    tok, q = (PART, SAMPLE) if it["sample"] else (it["tiles"][0] * P, P)
                    nt = len(it["tiles"])
                    for e in range(2):
                        half = slice(64 * e, 64 * e + 64)
                        src = ps_o[0:64, 0:n].rearrange("p (t e c) -> p t e c", t=nt, e=2)[:, :, e, :]
                        dst = og[half, 0:nt * q].rearrange("p (t c) -> p t c", t=nt)
                        gt = silu_g[half, hp, tok:tok + nt * q].rearrange("p (t c) -> p t c", t=nt)
                        last = V.scalar_tensor_tensor(out=dst, in0=src, scalar=0.5, in1=gt, op0=ALU.mult, op1=ALU.mult)
                    last.then_inc(og_ready, 1)
                elif kind == "FO":
                    _, p, t = st
                    if t % 2 == 1:
                        n = ft_at[(p, t)]
                        dve.wait_ge(out_turned, n + 1)
                        dve.wait_ge(rstd_ready, norms(p, 2))
                        rows_stored(dve, n % 4, n)
                        if n % 4 == 2:
                            dve.wait_ge(og_ready, sum(1 for x in items if x["p"] <= p))
                        if n % 4 == 3:
                            dve.wait_ge(max_ready, sum(1 for x in items if x["p"] <= p))
                            if p + 1 < PARTS:
                                dve.wait_ge(x_squared, xt_at[(p + 1, 1)] + 1)
                        V.tensor_scalar(out_rows[n % 4], t_flat, rstd[:, t:t + 1], None, ALU.mult).then_inc(out_dve, 1)

        @block.scalar
        def _(act):
            A = nc.scalar.activation
            act.wait_ge(prm_turned, 1)
            A(prm[:, :], t_flat[:, 0:R_ALL], ACT.Copy).then_inc(prm_ready, 1)
            act.wait_ge(prm_ready, 1)
            A(c_t[:, :], prm[:, R_C:R_C + 16], ACT.Tanh, scale=0.5).then_inc(c_tanh, 1)

            for st in steps:
                kind = st[0]
                if kind == "W":
                    j = st[1]
                    act.wait_ge(raw_loaded[j % 2], loads[j])
                    if j >= RING:
                        tile_used(act, j - RING)
                    A(w_hi[:, j % RING, 0:width[j]], w_raw[:, j % 2, 0:width[j]], ACT.Copy).then_inc(w_hi_ready, 1)
                elif kind == "MR":
                    m = st[1]
                    act.wait_ge(ada_done, KT * (m + 1))
                    if m:
                        act.wait_ge(mod_turned, m)
                    else:
                        act.wait_ge(prm_turned, 2)
                    for half in range(2):
                        last = A(mod_rows[:, 512 * half:512 * (half + 1)], mod_bank[m][half][0:2, :], ACT.Copy)
                    last.then_inc(mod_rows_ready, 1)
                elif kind == "XT":
                    _, p, t = st
                    n = xt_at[(p, t)]
                    c0, r0 = tok_span(t)
                    act.wait_ge(x_turned, n + 1)
                    if "act" in x_halves(p, t):
                        if p:
                            act.wait_ge(out_turned, ft_at[(p - 1, t + (p == 1 and t == TILES - 1))] + 1)
                        for half, bank in enumerate(x_banks(p, t)):
                            if x_halves(p, t)[half] == "act":
                                last = A(x_res[:, 4 * half:4 * half + 4, c0 + r0:c0 + P],
                                         bank[:, :].rearrange("p (k c) -> p k c", k=4)[:, :, 0:P - r0], ACT.Copy)
                        last.then_inc(x_put_act, 1)
                elif kind == "XS":
                    _, p, t = st
                    n = xt_at[(p, t)]
                    _, r0 = tok_span(t)
                    act.wait_ge(x_loaded[n % 2], 16 * (n // 2 + 1))
                    if n == 0:
                        act.wait_ge(dve_const, 1)
                    if p and t == 0:
                        act.wait_ge(var_ready, norms(p - 1, 0))
                        act.wait_ge(max_ready, sum(1 for x in items if x["p"] < p))
                        rows_stored(act, 3, ft_at[(p - 1, 0)])
                    if p == 0 or t > 1:
                        act.wait_ge(x_turned, n + 1)
                    if p and n > xt_at[(1, 0)]:
                        act.wait_ge(x_squared, n)
                    junk = bias_flat if p and t < 2 else x_in[r0:P, n % 2, :]
                    A(junk, x_in[r0:P, n % 2, :], ACT.Square, accum_out=ss[r0:P, t:t + 1]).then_inc(x_squared, 1)
                elif kind == "HS":
                    _, p, k = st
                    if k == 0:
                        act.wait_ge(x_put_dve, xt_dve[(p, TILES - 1)])
                        act.wait_ge(x_put_act, xt_act[(p, TILES if p == 0 else TILES - 1)])
                        act.wait_ge(mod_ready, mod_at[(0, 1)])
                    for c, w, v in spans(0, cols(p)):
                        last = A(h_hi[:, k, c:c + w], x_res[:, k, c:c + w], ACT.Copy, scale=gain[:, 0, k, v:v + 1])
                    last.then_inc(h_hi_ready, 1)
                elif kind == "NB":
                    _, p, r = st
                    act.wait_ge(rstd_spread, 2 * p + r + 1)
                    act.wait_ge(scaled, max([u["nth_proj"] for u in units if "nth_proj" in u and
                                             (u["p"] < p or (u["p"] == p and r and u["kind"] in ("u", "gate")))], default=0)) if (p or r) else None
                    last = A(rstd_b[:, 0:PART], ps_t[:, 0, :], ACT.Copy)
                    if p == 0:
                        last = A(rstd_b[:, PART:COLS], ps_t[:, 1, 0:SAMPLE], ACT.Copy)
                    last.then_inc(rb_ready, 1)
                elif kind == "E1":
                    u = units[st[1]]
                    p, c0, w, k = u["p"], u["c0"], u["w"], u["kind"]
                    bank = bank_of(u)
                    if k in ("u", "gate", "kv", "q", "agate"):
                        act.wait_ge(scaled, u["nth_proj"])
                        if k == "kv":
                            n = GROUPS * p + u["g"]
                            if n and u["b"] == 0:
                                act.wait_ge(v_turned, n)
                                act.wait_ge(k_lo_half, n)
                                act.wait_ge(k_prev, n)
                        if k == "u" and u["b"] == 0:
                            if u["p"] and u["g"] == 0 and u["i"] == 0:
                                act.wait_ge(rstd_spread, 2 * p + 1)
                            n = 8 * p + 2 * u["g"] + u["i"] - 1
                            if n >= 1:
                                act.wait_ge(pooled_ready, n)
                        for c, ww, v in spans(c0, w):
                            src = bank[:, c - c0:c - c0 + ww]
                            if k == "u":
                                at = c + U_PROMPT if v == 0 else c - PART + U_SAMPLE
                                dst = u_rows[u["i"]][:, at:at + ww]
                            elif k == "kv":
                                dst = kv_t[:, WINDOW + c:WINDOW + c + ww]
                            else:
                                dst = src
                            last = A(dst, src, ACT.Identity, bias=wb[:, u["n"], v:v + 1])
                        last.then_inc(biased, 1)
                        if k in ("gate", "agate"):
                            act.wait_ge(biased, u["nth_proj"])
                            if k == "gate":
                                n = 8 * p + 2 * u["g"] + u["i"]
                                before = [x for x in units if x["kind"] == "z" and 8 * x["p"] + x["n"] < n - 1 + 0 and x["u"] < u["u"]]
                                if before:
                                    act.wait_ge(y_ready, before[-1]["nth_z"])
                                if p and u["g"] == 0:
                                    rows_stored(act, 2, ft_at[(p - 1, TILES - 1 + (p == 1))] + 1)
                                    act.wait_ge(og_ready, sum(1 for x in items if x["p"] < p))
                            else:
                                act.wait_ge(y_ready, sum(1 for x in units if x["kind"] == "z" and x["p"] <= p))
                                before = [x["a"] for x in items if x["hp"] == u["i"] and (x["p"], x["g"]) < (p, u["g"])]
                                if before:
                                    act.wait_ge(og_ready, before[-1] + 1)
                            A(silu_g[:, u["i"], c0:c0 + w], bank[:, 0:w], ACT.Tanh, scale=0.5).then_inc(tanh_ready, 1)
                        elif k == "q":
                            act.wait_ge(biased, u["nth_proj"])
                            before = [x["a"] for x in items if x["hp"] == u["i"] and (x["p"], x["g"]) < (p, u["g"])]
                            if before:
                                act.wait_ge(s_ready, before[-1] + 1)
                            for e in range(2):
                                last = A(q_st[0:64, 2 * u["i"] + e, c0:c0 + w], bank[64 * e:64 * e + 64, 0:w], ACT.Copy)
                            last.then_inc(q_hi_ready, 1)
                    elif k == "z":
                        act.wait_ge(y_ready, u["nth_z"])
                        A(y_hi[:, u["n"], c0:c0 + w], acc[:, c0:c0 + w], ACT.Copy).then_inc(yz_hi, 1)
                    else:
                        l, n = u["layer"], u["n"]
                        if u["b"] == len(sched.blocks(p)) - 1:
                            act.wait_ge(x_new, u["nth_out"])
                            i = 16 * p + 8 * l + n
                            if 2 * p + l:
                                act.wait_ge(ssum_done, 2 * p + l)
                            if n:
                                act.wait_ge(acc_ready, (2 * p + l) * (KT - 1) + n)
                            elif l == 0:
                                act.wait_ge(yz_lo, sum(1 for x in units if x["kind"] == "z" and x["p"] <= p))
                            else:
                                act.wait_ge(yo_lo, sum(1 for x in items if x["p"] <= p))
                                act.wait_ge(og_ready, sum(1 for x in items if x["p"] <= p))
                            A(sq[:, 0:cols(p)], x_res[:, n, 0:cols(p)], ACT.Square).then_inc(sq_ready, 1)
                            if l == 0:
                                act.wait_ge(mod_ready, mod_at[(1, 1)])
                                for c, ww, v in spans(0, cols(p)):
                                    last = A(h_hi[:, n, c:c + ww], x_res[:, n, c:c + ww], ACT.Copy, scale=gain[:, 1, n, v:v + 1])
                                last.then_inc(h_hi_ready, 1)
                            else:
                                act.wait_ge(sq_ready, i + 1)
                                A(x_res[:, n, 0:cols(p)], x_res[:, n, 0:cols(p)], ACT.Copy,
                                  scale=prm[:, R_FINAL + n:R_FINAL + n + 1]).then_inc(x_scaled, 1)
                elif kind == "PL":
                    _, p, g, i = st
                    n = 8 * p + 2 * g + i
                    act.wait_ge(pooled_ready, n + 1)
                    A(q_st[:, i, 0:cols(p)], sq[:, 0:cols(p)], ACT.Copy).then_inc(pooled_hi, 1)
                elif kind == "PS":
                    p = st[1]
                    act.wait_ge(state_turned, 1 if p == 0 else 2)
                    nat_free(act, ("state", p))
                    A(nat[:, :], ps_o[:, 0:P], ACT.Copy).then_inc(state_nat, 1)
                elif kind == "KS":
                    _, p, g = st
                    d, n = g % 2, GROUPS * p + g + 1
                    act.wait_ge(k_prev, n)
                    before = [x["a"] for x in items if GROUPS * x["p"] + x["g"] <= n - 3]
                    if before:
                        act.wait_ge(s_ready, before[-1] + 1)
                    a = 0 if p else WINDOW
                    last = A(k_hi[0:64, d, a:K_CACHE], kv_t[0:64, a:K_CACHE], ACT.Copy)
                    if p == 0:
                        last = A(k_hi[0:64, d, K_NEW:K_COLS], kv_t[0:64, K_CACHE:K_CACHE + SAMPLE], ACT.Copy)
                    last.then_inc(k_hi_half, 1)
                elif kind == "VT":
                    _, p, g = st
                    d, n = g % 2, GROUPS * p + g + 1
                    act.wait_ge(v_turned, n)
                    before = [x["a"] for x in items if GROUPS * x["p"] + x["g"] <= n - 3]
                    if before:
                        act.wait_ge(pv_done, before[-1] + 1)
                    src = s_flat.rearrange("p (b c) -> p b c", c=P)
                    a = 0 if p else 1
                    m = TILES + 1 - a
                    last = A(v_st[:, d, a:TILES + 1, 0:64], src[:, 0:m, 64:128], ACT.Copy)
                    if p == 0:
                        r = slice(P - SAMPLE, P)
                        A(v_st[r, d, TILES + 2, 0:64], src[r, 5, 64:128], ACT.Copy)
                        A(v_st[:, d, TILES + 1, 0:64], kv_cache[:, g, 64:128], ACT.Copy)
                        last = A(k_hi[0:64, d, K_CACHE:K_NEW], src[0:64, 4, :], ACT.Copy)
                    last.then_inc(v_hi_ready, 1)
                    act.wait_ge(v_hi_ready, n)
                    act.wait_ge(k_hi_half, n)
                    a, e = (0, K_CACHE) if p else (WINDOW, K_COLS)
                    A(k_hi[64:128, d, a:e], k_hi[0:64, d, a:e].bitcast(F32), ACT.Copy).then_inc(k_hi_ready, 1)
                elif kind == "EX":
                    it = items[st[1]]
                    a, d = it["a"], it["a"] % 2
                    r = slice(P - SAMPLE, P) if it["sample"] else slice(0, P)
                    nb = 2 * len(it["tiles"])
                    act.wait_ge(max_ready, a + 1)
                    if a >= 2:
                        act.wait_ge(recip_ready, a - 1)
                    for at, t, e, k0 in item_blocks(it):
                        x = work[r, d, at * 256 + k0:at * 256 + (WINDOW + SAMPLE if it["sample"] else 256)]
                        A(x, x, ACT.Exp, bias=neg_max[r, d, at:at + 1], accum_out=row_sum[r, d, at:at + 1])
                    A(sink_exp[r, d, 0:nb], sink_arg[r, d, 0:nb], ACT.Exp).then_inc(sink_ready, 1)
                elif kind == "PH":
                    it = items[st[1]]
                    a = it["a"]
                    act.wait_ge(p_turned, a + 1)
                    if a:
                        act.wait_ge(pv_done, a)
                    o, e = span_of(it)
                    A(pt_hi[:, o:e], t_flat[:, o:e], ACT.Copy).then_inc(pt_hi_ready, 1)
                elif kind == "OG":
                    it = items[st[1]]
                    a, p = it["a"], it["p"]
                    n = 64 if it["sample"] else 512
                    act.wait_ge(pv_done, a + 1)
                    if a:
                        act.wait_ge(og_ready, a)
                    act.wait_ge(ssum_done, 2 * p + 1)
                    A(h_half[:, 0:n], ps_o[64:128, 0:n], ACT.Copy).then_inc(half_ready, 1)
                elif kind == "YH":
                    it = items[st[1]]
                    a, p = it["a"], it["p"]
                    act.wait_ge(og_ready, a + 1)
                    tok, q = (PART, SAMPLE) if it["sample"] else (it["tiles"][0] * P, P)
                    nt = len(it["tiles"])
                    A(y_hi[:, 2 * it["g"] + it["hp"], tok:tok + nt * q], og[:, 0:nt * q], ACT.Copy).then_inc(yo_hi, 1)
                elif kind == "FO":
                    _, p, t = st
                    if t % 2 == 0:
                        n = ft_at[(p, t)]
                        act.wait_ge(out_turned, n + 1)
                        act.wait_ge(rstd_ready, norms(p, 2))
                        rows_stored(act, n % 4, n)
                        if n % 4 == 2:
                            act.wait_ge(og_ready, sum(1 for x in items if x["p"] <= p))
                        if n % 4 == 3:
                            act.wait_ge(max_ready, sum(1 for x in items if x["p"] <= p))
                            if p + 1 < PARTS:
                                act.wait_ge(x_squared, xt_at[(p + 1, 1)] + 1)
                        A(out_rows[n % 4], s_flat, ACT.Copy, scale=rstd[:, t:t + 1]).then_inc(out_act, 1)

        @block.gpsimd
        def _(pool):
            G = nc.gpsimd
            G.memset(ident[:, :], 0.0).then_inc(pool_const, 1)
            pool.wait_ge(pool_const, 1)
            G.affine_select(out=ident[:, :], in_=ident[:, :], compare_op=ALU.not_equal, fill=1.0, base=0,
                            pattern=[[-1, P]], channel_multiplier=1).then_inc(pool_const, 1)
            G.iota(offsets.bitcast(I32), pattern=[[1, 2 * WINDOW]], base=-WINDOW, channel_multiplier=-1).then_inc(pool_const, 1)
            pool.wait_ge(dve_const, 2)
            split, biases, lows = 0, 0, 0
            for st in steps:
                kind = st[0]
                if kind == "W":
                    j = st[1]
                    split = j + 1
                    pool.wait_ge(w_hi_ready, j + 1)
                    pool.wait_ge(raw_loaded[j % 2], loads[j])
                    G.tensor_tensor(w_lo[:, j % RING, 0:width[j]], w_raw[:, j % 2, 0:width[j]],
                                    w_hi[:, j % RING, 0:width[j]].bitcast(F32), ALU.subtract).then_inc(w_lo_ready, 1)
                elif kind == "NA":
                    _, p, r = st
                    nt = TILES + (p == 0)
                    pool.wait_ge(var_ready, norms(p, r))
                    if p and r == 0:
                        f = ft_at[(p - 1, TILES - 1 + (p == 1))]
                        pool.wait_ge(out_act, sum(1 for x in ft[:f + 1] if x[2] % 2 == 0))
                        pool.wait_ge(out_dve, sum(1 for x in ft[:f + 1] if x[2] % 2 == 1))
                    if r:
                        pool.wait_ge(diag_ready, 2 * p + r)
                    G.tensor_tensor(rstd[:, 0:nt], var[:, 0:nt], power[:, 0:nt], ALU.pow).then_inc(rstd_ready, 1)
                elif kind == "E1" and units[st[1]]["kind"] == "out":
                    u = units[st[1]]
                    p, n = u["p"], u["n"]
                    if u["b"] == len(sched.blocks(p)) - 1 and n < KT - 1:
                        pool.wait_ge(sq_ready, 16 * p + 8 * u["layer"] + n + 1)
                        w = cols(p)
                        if n:
                            pool.wait_ge(acc_ready, (2 * p + u["layer"]) * (KT - 1) + n)
                            G.tensor_tensor(acc[:, 0:w], acc[:, 0:w], sq[:, 0:w], ALU.add).then_inc(acc_ready, 1)
                        else:
                            if u["layer"] == 1 or p:
                                pool.wait_ge(ssum_done, 2 * p + u["layer"])
                            G.tensor_copy(acc[:, 0:w], sq[:, 0:w]).then_inc(acc_ready, 1)
                elif kind == "BI":
                    _, p, g, hp = st
                    before = [x["a"] for x in items if x["hp"] == hp and (x["p"], x["g"]) < (p, g)]
                    pool.wait_ge(mod_turned, len(sched.mods))
                    pool.wait_ge(x_squared, xt_at[(p, TILES - 1)] + 1)
                    rows_stored(pool, 3, ft_at[(p, 0)])
                    if before:
                        pool.wait_ge(max_ready, before[-1] + 1)
                    for e in range(2):
                        last = G.tensor_scalar(bias[:, 2 * hp + e, :], dist[:, :], -slope(4 * g + 2 * hp + e) * HEAD_DIM ** 0.5, 0.0,
                                               ALU.mult, ALU.add)
                    last.then_inc(bias_ready, 1)
                    biases += 1
                elif kind == "YL":
                    it = items[st[1]]
                    a, g, hp = it["a"], it["g"], it["hp"]
                    tok, q = (PART, SAMPLE) if it["sample"] else (it["tiles"][0] * P, P)
                    nt = len(it["tiles"])
                    pool.wait_ge(og_ready, a + 1)
                    pool.wait_ge(yo_hi, a + 1)
                    yt = 2 * g + hp
                    G.tensor_tensor(y_lo[:, yt, tok:tok + nt * q], og[:, 0:nt * q], y_hi[:, yt, tok:tok + nt * q].bitcast(F32),
                                    ALU.subtract).then_inc(yo_lo, 1)
                    lows = a + 1
                elif kind == "SR":
                    it = items[st[1]]
                    a, d = it["a"], it["a"] % 2
                    pool.wait_ge(recip_ready, a + 1)
                    pool.wait_ge(sink_ready, a + 1)
                    r = slice(P - SAMPLE, P) if it["sample"] else slice(0, P)
                    if it["sample"]:
                        pool.wait_ge(w_lo_ready, split)
                        pool.wait_ge(norm_ready, a)
                        pool.wait_ge(bias_ready, biases)
                        if lows:
                            pool.wait_ge(yo_lo, lows)
                    for n, t in enumerate(it["tiles"]):
                        k0, w = (WINDOW, WINDOW) if (it["p"] == 0 and t == 0) else (0, 256)
                        if it["sample"]:
                            w = WINDOW + SAMPLE
                        x = work[r, d, n * 512:n * 512 + 512].rearrange("p (e c) -> p e c", e=2)[:, :, k0:k0 + w]
                        last = G.tensor_tensor(x, x, recip[r, d, 2 * n:2 * n + 2].unsqueeze(2).to_broadcast([r.stop - r.start, 2, w]), ALU.mult)
                    last.then_inc(norm_ready, 1)
                    if it["sample"]:
                        pool.wait_ge(norm_ready, a + 1)


_INS = ['x_prompt', 'x_sample', 'c_prompt', 'c_sample', 'cache_pool', 'cache_k', 'cache_v', 'norm_g', 'ada_w', 'ada_b',
        'pool_w_in', 'pool_w_grp', 'pool_scale', 'pool_w_out', 'attn_w_in', 'attn_sinks', 'attn_w_out', 'final_g']
_KV = (1, 1, WINDOW, 4, HEAD_DIM)
_OUTS = [(1, SEQ, D_MODEL), (1, SAMPLE, D_MODEL), (1, 1, HIST - 1, D_MODEL), _KV, _KV, (1, 1, HIST - 1, D_MODEL), _KV, _KV]


def kernel(**inputs):
    import numpy as _np
    import concourse.bacc as _bacc
    from concourse.bass_utils import run_bass_kernel_spmd as _run

    nc = _bacc.Bacc("TRN2", target_bir_lowering=False, num_devices=1)
    arrays, ins = {}, {}
    for name in _INS:
        a = _np.ascontiguousarray(inputs[name])
        arrays[f"in_{name}_dram"] = a
        ins[name] = nc.dram_tensor(f"in_{name}_dram", a.shape, mybir.dt.from_np(a.dtype), kind="ExternalInput").ap()
    outs = [nc.dram_tensor(f"out_{i}_dram", shape, F32, kind="ExternalOutput").ap() for i, shape in enumerate(_OUTS)]
    trunk_kernel(nc, ins, outs)
    r = _run(nc, [arrays], core_ids=[0])
    return tuple(r.results[0][f"out_{i}_dram"] for i in range(len(_OUTS)))
```
